# Optimizing a Trainium2 kernel written in Bass

```python
import math
import jax, jax.numpy as jnp
from jax import lax
import numpy as np

D_MODEL = 1024
BATCH = 1
SEQ = 256
DEPTH = 1

D_MIX = D_MODEL
N_HEADS_A = 8
HEAD_DIM_A = 64
DIL_CONFIGS = ((128, 1), (512, 4), (2048, 16))
Q_BLOCK = 128
N_HEADS_B = 8
QK_NOPE = 64
QK_ROPE = 32
V_DIM = 64
Q_LORA = 384
KV_LORA = 256
ROPE_BASE = 10000.0
D_FF = 2816
CONV_WIDTH = 3
EPS = 1e-6
NEG = -1e30

WIDTH_A = N_HEADS_A * HEAD_DIM_A
WIDTH_B = N_HEADS_B * V_DIM
IN_SIZES = (WIDTH_A, WIDTH_A, WIDTH_A, Q_LORA, KV_LORA, QK_ROPE)
D_IN = sum(IN_SIZES)
SPLIT_POINTS = tuple(int(v) for v in np.cumsum(IN_SIZES)[:-1])


def _rmsnorm(x, g):
    xf = x.astype(jnp.float32)
    y = xf * lax.rsqrt(jnp.mean(xf * xf, axis=-1, keepdims=True) + EPS)
    return (y * g.astype(jnp.float32)).astype(x.dtype)

def _rope(x, cos, sin):
    xf = x.astype(jnp.float32)
    half = xf.shape[-1] // 2
    x1, x2 = xf[..., :half], xf[..., half:]
    out = jnp.concatenate([x1 * cos - x2 * sin, x2 * cos + x1 * sin], axis=-1)
    return out.astype(x.dtype)

def _dilated_branch(q, k, v, slopes, window, dilation):
    b, h, s, d = q.shape
    r = dilation
    half = window // (2 * dilation)
    L = s // r
    qb = min(Q_BLOCK, L)
    nblk = -(-L // qb)
    Lp = nblk * qb
    slab = qb + 2 * half

    def to_dilated(t):
        return t.reshape(b, h, L, r, d).transpose(0, 1, 3, 2, 4)

    qd, kd, vd = to_dilated(q), to_dilated(k), to_dilated(v)
    qd = jnp.pad(qd, ((0, 0), (0, 0), (0, 0), (0, Lp - L), (0, 0)))
    pad_kv = ((0, 0), (0, 0), (0, 0), (half, half + Lp - L), (0, 0))
    kd = jnp.pad(kd, pad_kv)
    vd = jnp.pad(vd, pad_kv)
    idx = jnp.arange(nblk)[:, None] * qb + jnp.arange(slab)[None, :]
    k_s = kd[:, :, :, idx, :].astype(jnp.float32)
    v_s = vd[:, :, :, idx, :].astype(jnp.float32)
    q_s = qd.reshape(b, h, r, nblk, qb, d).astype(jnp.float32)

    scores = jnp.einsum('bhcnqd,bhcnkd->bhcnqk', q_s, k_s) * (d ** -0.5)
    off = jnp.arange(slab)[None, :] - half - jnp.arange(qb)[:, None]
    key_pos = idx - half
    valid = (jnp.abs(off) <= half)[None, :, :] & ((key_pos >= 0) & (key_pos < L))[:, None, :]
    dist = (jnp.abs(off) * r).astype(jnp.float32)
    alibi = -slopes[:, None, None] * dist[None]
    scores = scores + alibi[None, :, None, None]
    scores = jnp.where(valid[None, None, None], scores, NEG)
    lse = jax.nn.logsumexp(scores, axis=-1)
    p = jnp.exp(scores - lse[..., None])
    o = jnp.einsum('bhcnqk,bhcnkd->bhcnqd', p, v_s)

    o = o.reshape(b, h, r, Lp, d)[:, :, :, :L].transpose(0, 1, 3, 2, 4).reshape(b, h, s, d)
    lse = lse.reshape(b, h, r, Lp)[:, :, :, :L].transpose(0, 1, 3, 2).reshape(b, h, s)
    return o, lse

def _dilated_attention(qa, ka, va):
    b, s, _ = qa.shape
    def heads(t):
        return t.reshape(b, s, N_HEADS_A, HEAD_DIM_A).transpose(0, 2, 1, 3)
    q, k, v = heads(qa), heads(ka), heads(va)
    slopes = jnp.exp2(-8.0 * jnp.arange(1, N_HEADS_A + 1, dtype=jnp.float32) / N_HEADS_A)
    outs, lses = [], []
    for window, dilation in DIL_CONFIGS:
        o, lse = _dilated_branch(q, k, v, slopes, window, dilation)
        outs.append(o)
        lses.append(lse)
    w = jax.nn.softmax(jnp.stack(lses, axis=0), axis=0)
    o = jnp.einsum('gbhs,gbhsd->bhsd', w, jnp.stack(outs, axis=0))
    return o.transpose(0, 2, 1, 3).reshape(b, s, WIDTH_A).astype(qa.dtype)

def _mla(c_q, c_kv, k_r, q_lat_norm, w_uq, kv_lat_norm, w_ukv):
    b, s, _ = c_q.shape
    pos = jnp.arange(s, dtype=jnp.float32)
    inv_freq = jnp.exp(-math.log(ROPE_BASE) * jnp.arange(0, QK_ROPE, 2, dtype=jnp.float32) / QK_ROPE)
    ang = pos[:, None] * inv_freq[None, :]
    cos, sin = jnp.cos(ang), jnp.sin(ang)

    q = (_rmsnorm(c_q, q_lat_norm) @ w_uq).reshape(b, s, N_HEADS_B, QK_NOPE + QK_ROPE)
    q_nope = q[..., :QK_NOPE]
    q_rope = _rope(q[..., QK_NOPE:], cos[:, None, :], sin[:, None, :])
    kv = (_rmsnorm(c_kv, kv_lat_norm) @ w_ukv).reshape(b, s, N_HEADS_B, QK_NOPE + V_DIM)
    k_nope = kv[..., :QK_NOPE].transpose(0, 2, 1, 3).astype(jnp.float32)
    v = kv[..., QK_NOPE:].transpose(0, 2, 1, 3).astype(jnp.float32)
    k_rope = _rope(k_r, cos, sin).astype(jnp.float32)
    scale = (QK_NOPE + QK_ROPE) ** -0.5

    nq = s // Q_BLOCK
    qn_blk = q_nope.reshape(b, nq, Q_BLOCK, N_HEADS_B, QK_NOPE).transpose(1, 0, 3, 2, 4)
    qr_blk = q_rope.reshape(b, nq, Q_BLOCK, N_HEADS_B, QK_ROPE).transpose(1, 0, 3, 2, 4)

    def block(args):
        qn, qr = args
        sc = (jnp.einsum('bhqd,bhkd->bhqk', qn.astype(jnp.float32), k_nope)
              + jnp.einsum('bhqr,bkr->bhqk', qr.astype(jnp.float32), k_rope)) * scale
        p = jax.nn.softmax(sc, axis=-1)
        return jnp.einsum('bhqk,bhkd->bhqd', p, v)

    o = lax.map(block, (qn_blk, qr_blk))
    return o.transpose(1, 0, 3, 2, 4).reshape(b, s, WIDTH_B).astype(c_q.dtype)

def _dwconv(u, w, bias):
    c = u.shape[-1]
    y = lax.conv_general_dilated(
        u, w[:, None, :].astype(u.dtype), window_strides=(1,),
        padding=((CONV_WIDTH // 2, CONV_WIDTH // 2),),
        dimension_numbers=('NWC', 'WIO', 'NWC'), feature_group_count=c)
    return y + bias.astype(u.dtype)

def first_inputs(seed: int = 0) -> dict:
    key = jax.random.key(seed)
    ks = jax.random.split(key, 17)
    f32 = jnp.float32

    def gain(k, n):
        return 1.0 + 0.1 * jax.random.normal(k, (DEPTH, n), f32)

    def dense(k, fan_in, fan_out):
        return jax.random.normal(k, (DEPTH, fan_in, fan_out), f32) * fan_in ** -0.5

    return {
        "x": jax.random.normal(ks[0], (BATCH, SEQ, D_MODEL), f32),
        "norm_mix_pre": gain(ks[1], D_MODEL),
        "w_in": dense(ks[2], D_MODEL, D_IN),
        "q_lat_norm": gain(ks[3], Q_LORA),
        "w_uq": dense(ks[4], Q_LORA, N_HEADS_B * (QK_NOPE + QK_ROPE)),
        "kv_lat_norm": gain(ks[5], KV_LORA),
        "w_ukv": dense(ks[6], KV_LORA, N_HEADS_B * (QK_NOPE + V_DIM)),
        "out_norm_a": gain(ks[7], WIDTH_A),
        "out_norm_b": gain(ks[8], WIDTH_B),
        "w_o": dense(ks[9], D_MIX, D_MODEL),
        "norm_mix_post": gain(ks[10], D_MODEL),
        "norm_ffn_pre": gain(ks[11], D_MODEL),
        "w_up": dense(ks[12], D_MODEL, 2 * D_FF),
        "conv_w": jax.random.normal(ks[13], (DEPTH, CONV_WIDTH, 2 * D_FF), f32) * CONV_WIDTH ** -0.5,
        "conv_b": 0.02 * jax.random.normal(ks[14], (DEPTH, 2 * D_FF), f32),
        "w_down": dense(ks[15], D_FF, D_MODEL),
        "norm_ffn_post": gain(ks[16], D_MODEL),
    }

def first_block(x, norm_mix_pre, w_in, q_lat_norm, w_uq, kv_lat_norm, w_ukv, out_norm_a,
              out_norm_b, w_o, norm_mix_post, norm_ffn_pre, w_up, conv_w, conv_b, w_down,
              norm_ffn_post):
    for l in range(DEPTH):
        h = _rmsnorm(x, norm_mix_pre[l])
        proj = h @ w_in[l]
        qa, ka, va, c_q, c_kv, k_r = jnp.split(proj, SPLIT_POINTS, axis=-1)
        ya = _dilated_attention(qa, ka, va)
        yb = _mla(c_q, c_kv, k_r, q_lat_norm[l], w_uq[l], kv_lat_norm[l], w_ukv[l])
        y = jnp.concatenate([_rmsnorm(ya, out_norm_a[l]), _rmsnorm(yb, out_norm_b[l])], axis=-1)
        y = y @ w_o[l]
        x = x + _rmsnorm(y, norm_mix_post[l])
        h = _rmsnorm(x, norm_ffn_pre[l])
        u = _dwconv(h @ w_up[l], conv_w[l], conv_b[l])
        g, v = u[..., :D_FF], u[..., D_FF:]
        y = (jax.nn.gelu(g, approximate=True) * v) @ w_down[l]
        x = x + _rmsnorm(y, norm_ffn_post[l])
    return x


DEPTH_2 = 4

N_MIXERS = 3
GRID_W = 64
CONV_WIDTH_2 = 31
NAT_HEADS = 16
NAT_HEAD_DIM = D_MODEL // NAT_HEADS
NAT_MAX_KH = 8
NAT_KW = 16
RET_HEADS = 4
RET_KEY_DIM = D_MODEL // RET_HEADS
RET_VAL_DIM = 2 * RET_KEY_DIM
RET_CHUNK = 128
RET_ROPE_BASE = 10000.0
FFN_DIM = ((8 * D_MODEL // 3 + 127) // 128) * 128
FFN_CONV_WIDTH = 3
N_CONV_LAYERS = (DEPTH_2 + 2) // 3
N_NAT_LAYERS = (DEPTH_2 + 1) // 3
N_RET_LAYERS = DEPTH_2 // 3


def rmsnorm(x, g):
    xf = x.astype(jnp.float32)
    y = xf * lax.rsqrt(jnp.mean(xf * xf, axis=-1, keepdims=True) + EPS)
    return y.astype(x.dtype) * g

def layernorm(x, g, b):
    xf = x.astype(jnp.float32)
    mu = jnp.mean(xf, axis=-1, keepdims=True)
    var = jnp.mean(jnp.square(xf - mu), axis=-1, keepdims=True)
    y = (xf - mu) * lax.rsqrt(var + EPS)
    return y.astype(x.dtype) * g + b

def dwconv(x, w, b):
    k, c = w.shape
    y = lax.conv_general_dilated(
        x, w[:, None, :].astype(x.dtype), window_strides=(1,),
        padding=[(k // 2, k // 2)], dimension_numbers=('NWC', 'WIO', 'NWC'),
        feature_group_count=c)
    return y + b

def conv_module(h, w_in, b_in, dw_w, dw_b, ln_g, ln_b, w_out):
    a, gt = jnp.split(h @ w_in + b_in, 2, axis=-1)
    u = a * jax.nn.sigmoid(gt)
    u = dwconv(u, dw_w, dw_b)
    u = layernorm(u, ln_g, ln_b)
    return jax.nn.silu(u) @ w_out

def nat_mixer(h, w_qkv, q_g, k_g, rpb, w_out):
    b, s, _ = h.shape
    rows = s // GRID_W
    kh = min(NAT_MAX_KH, rows)
    qkv = (h @ w_qkv).reshape(b, s, 3, NAT_HEADS, NAT_HEAD_DIM)
    q = rmsnorm(qkv[:, :, 0], q_g) * (NAT_HEAD_DIM ** -0.5)
    k = rmsnorm(qkv[:, :, 1], k_g)
    v = qkv[:, :, 2]

    def to_grid(t):
        return t.reshape(b, rows, GRID_W, NAT_HEADS, NAT_HEAD_DIM).transpose(0, 3, 1, 2, 4)

    qg, kg, vg = to_grid(q), to_grid(k), to_grid(v)
    cols = jnp.arange(GRID_W)
    col_start = jnp.clip(cols - NAT_KW // 2, 0, GRID_W - NAT_KW)
    col_idx = col_start[:, None] + jnp.arange(NAT_KW)[None, :]
    dc_idx = col_idx - cols[:, None] + (NAT_KW - 1)

    def row_fn(r):
        rs = jnp.clip(r - kh // 2, 0, rows - kh)
        q_r = lax.dynamic_index_in_dim(qg, r, axis=2, keepdims=False)
        k_win = lax.dynamic_slice_in_dim(kg, rs, kh, axis=2)[:, :, :, col_idx]
        v_win = lax.dynamic_slice_in_dim(vg, rs, kh, axis=2)[:, :, :, col_idx]
        dr_idx = rs + jnp.arange(kh) - r + (NAT_MAX_KH - 1)
        bias = rpb[:, dr_idx[:, None, None], dc_idx[None, :, :]]
        sc = jnp.einsum('bhqd,bhrqwd->bhqrw', q_r, k_win).astype(jnp.float32)
        sc = sc + bias.transpose(0, 2, 1, 3)[None].astype(jnp.float32)
        p = jax.nn.softmax(sc.reshape(b, NAT_HEADS, GRID_W, kh * NAT_KW), axis=-1)
        p = p.reshape(b, NAT_HEADS, GRID_W, kh, NAT_KW).astype(v_win.dtype)
        return jnp.einsum('bhqrw,bhrqwd->bhqd', p, v_win)

    out = lax.map(row_fn, jnp.arange(rows))
    out = out.transpose(1, 0, 3, 2, 4).reshape(b, s, D_MODEL)
    return out @ w_out

def rotary(x):
    s, d = x.shape[1], x.shape[-1]
    half = d // 2
    theta = 1.0 / (RET_ROPE_BASE ** jnp.linspace(0.0, 1.0, half, dtype=jnp.float32))
    ang = jnp.arange(s, dtype=jnp.float32)[:, None] * theta[None, :]
    cos, sin = jnp.cos(ang)[:, None, :], jnp.sin(ang)[:, None, :]
    x1, x2 = x[..., :half].astype(jnp.float32), x[..., half:].astype(jnp.float32)
    return jnp.concatenate([x1 * cos - x2 * sin, x1 * sin + x2 * cos], axis=-1)

def retention_scan(q, k, v, log_gamma, include_diag):
    b, h, s, dk = q.shape
    dv = v.shape[-1]
    nc = s // RET_CHUNK

    def chunks(t):
        return jnp.moveaxis(t.reshape(b, h, nc, RET_CHUNK, t.shape[-1]), 2, 0)

    pos = jnp.arange(RET_CHUNK, dtype=jnp.float32)
    diff = pos[:, None] - pos[None, :]
    mask = (diff >= 0) if include_diag else (diff > 0)
    expo = jnp.where(mask, diff, 0.0)[None] * log_gamma[:, None, None]
    decay_intra = jnp.where(mask[None], jnp.exp(expo), 0.0)
    q_decay = jnp.exp((pos + 1.0)[None, :] * log_gamma[:, None])
    k_decay = jnp.exp((RET_CHUNK - 1.0 - pos)[None, :] * log_gamma[:, None])
    chunk_decay = jnp.exp(RET_CHUNK * log_gamma)

    def step(state, inp):
        qc, kc, vc = inp
        inter = jnp.einsum('bhcd,bhde->bhce', qc, state) * q_decay[None, :, :, None]
        sc = jnp.einsum('bhid,bhjd->bhij', qc, kc) * decay_intra[None]
        out = inter + jnp.einsum('bhij,bhje->bhie', sc, vc)
        state = state * chunk_decay[None, :, None, None] + jnp.einsum(
            'bhjd,bhje->bhde', kc * k_decay[None, :, :, None], vc)
        return state, out

    state0 = jnp.zeros((b, h, dk, dv), jnp.float32)
    _, outs = lax.scan(step, state0, (chunks(q), chunks(k), chunks(v)))
    return jnp.moveaxis(outs, 0, 2).reshape(b, h, s, dv)

def retention_mixer(h, w_in, log2_inv_decay, gn_g, w_out):
    b, s, _ = h.shape
    hk = RET_HEADS * RET_KEY_DIM
    hv = RET_HEADS * RET_VAL_DIM
    q, k, v, g = jnp.split(h @ w_in, [hk, 2 * hk, 2 * hk + hv], axis=-1)
    q = rotary(q.reshape(b, s, RET_HEADS, RET_KEY_DIM)).transpose(0, 2, 1, 3)
    k = (rotary(k.reshape(b, s, RET_HEADS, RET_KEY_DIM)) * (RET_KEY_DIM ** -0.5)).transpose(0, 2, 1, 3)
    v = v.reshape(b, s, RET_HEADS, RET_VAL_DIM).transpose(0, 2, 1, 3).astype(jnp.float32)
    log_gamma = jnp.log1p(-jnp.exp2(-log2_inv_decay.astype(jnp.float32)))
    o_fwd = retention_scan(q, k, v, log_gamma[0], True)
    o_bwd = jnp.flip(retention_scan(jnp.flip(q, 2), jnp.flip(k, 2), jnp.flip(v, 2),
                                    log_gamma[1], False), 2)
    o = (o_fwd + o_bwd).transpose(0, 2, 1, 3)
    mu = jnp.mean(o, axis=-1, keepdims=True)
    var = jnp.mean(jnp.square(o - mu), axis=-1, keepdims=True)
    o = ((o - mu) * lax.rsqrt(var + EPS)).reshape(b, s, hv).astype(h.dtype) * gn_g
    return (jax.nn.silu(g) * o) @ w_out

def conv_ffn(h, w_up, dw_w, dw_b, w_down):
    u = dwconv(h @ w_up, dw_w, dw_b)
    val, gate = jnp.split(u, 2, axis=-1)
    return (jax.nn.gelu(gate) * val) @ w_down

def second_inputs(seed: int = 0) -> dict:
    key = jax.random.key(seed)
    ks = iter(jax.random.split(key, 32))
    f32 = jnp.float32
    D = D_MODEL

    def nrm(shape, scale):
        return jax.random.normal(next(ks), shape, f32) * scale

    def gain(shape):
        return 1.0 + nrm(shape, 0.02)

    ret_in = 2 * RET_HEADS * RET_KEY_DIM + 2 * RET_HEADS * RET_VAL_DIM
    hv = RET_HEADS * RET_VAL_DIM
    decay_base = 5.0 + jnp.arange(RET_HEADS, dtype=f32)
    return {
        'x': nrm((BATCH, SEQ, D), 1.0),
        'norm1_g': gain((DEPTH_2, D)),
        'norm2_g': gain((DEPTH_2, D)),
        'conv_w_in': nrm((N_CONV_LAYERS, D, 2 * D), D ** -0.5),
        'conv_b_in': nrm((N_CONV_LAYERS, 2 * D), 0.02),
        'conv_dw_w': nrm((N_CONV_LAYERS, CONV_WIDTH_2, D), CONV_WIDTH_2 ** -0.5),
        'conv_dw_b': nrm((N_CONV_LAYERS, D), 0.02),
        'conv_ln_g': gain((N_CONV_LAYERS, D)),
        'conv_ln_b': nrm((N_CONV_LAYERS, D), 0.02),
        'conv_w_out': nrm((N_CONV_LAYERS, D, D), D ** -0.5),
        'nat_w_qkv': nrm((N_NAT_LAYERS, D, 3 * D), D ** -0.5),
        'nat_q_norm_g': gain((N_NAT_LAYERS, NAT_HEAD_DIM)),
        'nat_k_norm_g': gain((N_NAT_LAYERS, NAT_HEAD_DIM)),
        'nat_rpb': nrm((N_NAT_LAYERS, NAT_HEADS, 2 * NAT_MAX_KH - 1, 2 * NAT_KW - 1), 0.02),
        'nat_w_out': nrm((N_NAT_LAYERS, D, D), D ** -0.5),
        'ret_w_in': nrm((N_RET_LAYERS, D, ret_in), D ** -0.5),
        'ret_log2_inv_decay': decay_base[None, None, :] + nrm((N_RET_LAYERS, 2, RET_HEADS), 0.1),
        'ret_gn_g': gain((N_RET_LAYERS, hv)),
        'ret_w_out': nrm((N_RET_LAYERS, hv, D), hv ** -0.5),
        'ffn_w_up': nrm((DEPTH_2, D, 2 * FFN_DIM), D ** -0.5),
        'ffn_dw_w': nrm((DEPTH_2, FFN_CONV_WIDTH, 2 * FFN_DIM), FFN_CONV_WIDTH ** -0.5),
        'ffn_dw_b': nrm((DEPTH_2, 2 * FFN_DIM), 0.02),
        'ffn_w_down': nrm((DEPTH_2, FFN_DIM, D), FFN_DIM ** -0.5),
    }

def second_block(x, norm1_g, norm2_g, conv_w_in, conv_b_in, conv_dw_w, conv_dw_b,
              conv_ln_g, conv_ln_b, conv_w_out, nat_w_qkv, nat_q_norm_g,
              nat_k_norm_g, nat_rpb, nat_w_out, ret_w_in, ret_log2_inv_decay,
              ret_gn_g, ret_w_out, ffn_w_up, ffn_dw_w, ffn_dw_b, ffn_w_down):
    for i in range(DEPTH_2):
        mixer, j = i % N_MIXERS, i // N_MIXERS
        h = rmsnorm(x, norm1_g[i])
        if mixer == 0:
            y = conv_module(h, conv_w_in[j], conv_b_in[j], conv_dw_w[j], conv_dw_b[j],
                            conv_ln_g[j], conv_ln_b[j], conv_w_out[j])
        elif mixer == 1:
            y = nat_mixer(h, nat_w_qkv[j], nat_q_norm_g[j], nat_k_norm_g[j],
                          nat_rpb[j], nat_w_out[j])
        else:
            y = retention_mixer(h, ret_w_in[j], ret_log2_inv_decay[j], ret_gn_g[j],
                                ret_w_out[j])
        x = x + y.astype(x.dtype)
        h = rmsnorm(x, norm2_g[i])
        x = x + conv_ffn(h, ffn_w_up[i], ffn_dw_w[i], ffn_dw_b[i], ffn_w_down[i]).astype(x.dtype)
    return x


def setup_inputs(seed=0):
    out = dict(first_inputs(seed))
    for name, value in second_inputs(seed + 1).items():
        if name != "x":
            out[name + "_2"] = value
    return out


def reference(
    x, norm_mix_pre, w_in, q_lat_norm, w_uq, kv_lat_norm, w_ukv, out_norm_a, out_norm_b, w_o,
    norm_mix_post, norm_ffn_pre, w_up, conv_w, conv_b, w_down, norm_ffn_post, norm1_g_2,
    norm2_g_2, conv_w_in_2, conv_b_in_2, conv_dw_w_2, conv_dw_b_2, conv_ln_g_2, conv_ln_b_2,
    conv_w_out_2, nat_w_qkv_2, nat_q_norm_g_2, nat_k_norm_g_2, nat_rpb_2, nat_w_out_2,
    ret_w_in_2, ret_log2_inv_decay_2, ret_gn_g_2, ret_w_out_2, ffn_w_up_2, ffn_dw_w_2,
    ffn_dw_b_2, ffn_w_down_2,
):
    x = first_block(
        x, norm_mix_pre, w_in, q_lat_norm, w_uq, kv_lat_norm, w_ukv, out_norm_a, out_norm_b,
        w_o, norm_mix_post, norm_ffn_pre, w_up, conv_w, conv_b, w_down, norm_ffn_post,
    )
    return second_block(
        x, norm1_g_2, norm2_g_2, conv_w_in_2, conv_b_in_2, conv_dw_w_2, conv_dw_b_2,
        conv_ln_g_2, conv_ln_b_2, conv_w_out_2, nat_w_qkv_2, nat_q_norm_g_2, nat_k_norm_g_2,
        nat_rpb_2, nat_w_out_2, ret_w_in_2, ret_log2_inv_decay_2, ret_gn_g_2, ret_w_out_2,
        ffn_w_up_2, ffn_dw_w_2, ffn_dw_b_2, ffn_w_down_2,
    )


_drawn_inputs = setup_inputs


def setup_inputs(seed=0):
    import zlib

    import numpy as np

    out = dict(_drawn_inputs(seed))
    spreads = {}
    factors = {'norm1_g_2': 3.119,
     'norm2_g_2': 2.817,
     'conv_b_in_2': 4.588,
     'conv_ln_g_2': 4.291,
     'conv_ln_b_2': 4.737,
     'nat_q_norm_g_2': 8.0,
     'nat_k_norm_g_2': 8.0,
     'nat_rpb_2': 27.493,
     'ret_gn_g_2': 23.667,
     'ffn_dw_b_2': 2.773}
    for name, (base, spread) in spreads.items():
        noise = np.random.default_rng([zlib.crc32(name.encode()), seed]).standard_normal(out[name].shape)
        drawn = base * np.exp(spread * noise) if base else spread * noise
        out[name] = __import__('jax').numpy.asarray(drawn.astype(out[name].dtype))
    for name, factor in factors.items():
        out[name] = (out[name] * factor).astype(out[name].dtype)
    return out
```

```python
import math

import numpy as np

import concourse.bass as bass
from concourse import mybir
from collections import Counter
from contextlib import ExitStack

F32 = mybir.dt.float32
F32R = mybir.dt.float32r
ACT = mybir.ActivationFunctionType
ALU = mybir.AluOpType
AX = mybir.AxisListType

P = 128
S = 256
D = 1024
DT = D // P
CH = 2048
RING = 3
FF = 2816
FT = FF // P
EPS = 1e-6
NEG = -1e30
HA, HDA = 8, 64
HB, NOPE, ROPE = 8, 64, 32
QL, KL = 384, 256
NH, NHD = 16, 64
GW, KW = 64, 16
GR = S // GW
RH, RKD, RVD = 4, 256, 512
CW = 31
PADC = CW // 2
PE_TAPS = (11, 11, 11, 11, 11, 11, 14, 14)

ALL_STAGES = ("mix", "ffn0", "conv0", "ffn1", "nat", "ffn2", "ret", "ffn3", "conv1", "ffn4")


def chunk_widths(name):
    if name == "mix":
        return [CH] * 9 + [2 * 3 * P] * 4 + [2 * 2 * P] * 4 + [2 * 256] * 2 + [CH] * 4
    if name.startswith("ffn"):
        return [CH] * (FT + FT // 2)
    if name.startswith("conv"):
        return [CH] * (8 + 4)
    if name == "nat":
        return [CH] * (8 + 4 + 4)
    return [CH] * (8 + 8 + 8 + 8)


def param_layout():
    at, off = {}, 0
    for name, n in (("norm_mix_pre", 8), ("q_lat_norm", 3), ("kv_lat_norm", 2), ("out_norm_a", 4),
                    ("out_norm_b", 4), ("norm_mix_post", 8), ("norm_ffn_pre", 8), ("norm_ffn_post", 8),
                    ("norm1_g_2", 32), ("norm2_g_2", 32), ("conv_b_in_2", 32), ("conv_dw_w_2", 2 * 8 * CW),
                    ("conv_dw_b_2", 16), ("conv_ln_g_2", 16), ("conv_ln_b_2", 16), ("nat_q_norm_g_2", 1),
                    ("nat_k_norm_g_2", 1), ("ret_log2_inv_decay_2", 8), ("ret_gn_g_2", 16),
                    ("ffn_dw", 5 * FT * 2 * 4)):
        at[name] = off
        off += n
    return at, off


def const_layout():
    at, off = {}, 0
    for name, n in (("ident", P), ("ones", P), ("half_ones", P), ("rope_cos", S), ("rope_sin", S),
                    ("rot_cos", S), ("rot_sin", S), ("fwd", 2 * S), ("bwd", 2 * S), ("nat_mask", GW), ("flip", P)):
        at[name] = off
        off += n
    return at, off


def build_constants():
    at, n = const_layout()
    c = np.zeros((P, n), np.float32)
    c[:, at["ident"]:at["ident"] + P] = np.eye(P)
    c[:, at["ones"]:at["ones"] + P] = 1.0
    for g in range(2):
        c[64 * g:64 * g + 64, at["half_ones"] + 64 * g:at["half_ones"] + 64 * g + 64] = 1.0
        flip = slice(at["flip"] + 64 * g, at["flip"] + 64 * g + 64)
        c[64 * g:64 * g + 64, flip] = np.eye(64)[::-1]
    pos = np.arange(S, dtype=np.float32)
    inv = np.exp(np.float32(-math.log(10000.0)) * np.arange(0, ROPE, 2, dtype=np.float32) / np.float32(ROPE)).astype(np.float32)
    ang = (pos[:, None] * inv[None, :]).astype(np.float32).T
    cos, sin = np.cos(ang).astype(np.float32), np.sin(ang).astype(np.float32)
    c[64:96, at["rope_cos"]:at["rope_cos"] + S] = np.concatenate([cos, cos])
    c[96:128, at["rope_sin"]:at["rope_sin"] + S] = np.concatenate([-sin, sin])
    theta = (1.0 / (np.float32(10000.0) ** np.linspace(0.0, 1.0, 128, dtype=np.float32))).astype(np.float32)
    ang = (pos[:, None] * theta[None, :]).astype(np.float32).T
    c[:, at["rot_cos"]:at["rot_cos"] + S] = np.cos(ang)
    c[:, at["rot_sin"]:at["rot_sin"] + S] = np.sin(ang)
    j = np.arange(S)[:, None]
    i = np.arange(S)[None, :]
    for name, m in (("fwd", np.maximum(i - j, 0)), ("bwd", np.maximum(j - i, 0))):
        c[:, at[name]:at[name] + 2 * S] = m.reshape(2, P, S).transpose(1, 0, 2).reshape(P, 2 * S)
    col = np.arange(GW)
    start = np.clip(col - KW // 2, 0, GW - KW)
    inside = (col[None, :] >= start[:, None]) & (col[None, :] < start[:, None] + KW)
    c[:, at["nat_mask"]:at["nat_mask"] + GW] = np.tile(np.where(inside, 0.0, NEG)[::-1], (2, 1))
    return c


def dilated_bias():
    t, s = np.arange(S)[:, None], np.arange(S)[None, :]
    dist = np.abs(t - s)
    count = np.zeros((S, S))
    for window, r in ((128, 1), (512, 4), (2048, 16)):
        count += (dist % r == 0) & (dist // r <= window // (2 * r))
    log_count = np.where(count > 0, np.log(np.maximum(count, 1)), NEG)
    out = np.empty((P, HA, 2, S), np.float32)
    for h in range(HA):
        slope = 2.0 ** (-8.0 * (h + 1) / HA)
        out[:, h] = (-slope * dist + log_count).reshape(2, P, S).transpose(1, 0, 2)
    return out.reshape(P, -1)


def build_program(nc, wstream, x_in, params_in, consts_in, bias_in, rpb_in, out, stages=ALL_STAGES):
    PA, NP_ = param_layout()
    CA, NC_ = const_layout()
    widths, first_chunk = [], {}
    for name in stages:
        first_chunk[name] = len(widths)
        widths += chunk_widths(name)
    n_used = len(widths)
    widths.append(CH)
    n_chunks = len(widths)

    with ExitStack() as ctx:
        def sb(name, shape, dt=F32):
            return ctx.enter_context(nc.sbuf_tensor(name, shape, dt))

        def sem(name):
            return ctx.enter_context(nc.semaphore(name))

        raw = sb("raw", [P, RING, CH])
        w_hi = sb("w_hi", [P, RING, CH], F32R)
        w_lo = sb("w_lo", [P, RING, CH], F32R)
        x = sb("x", [P, DT, S])
        h_hi = sb("h_hi", [P, 16, S], F32R)
        h_lo = sb("h_lo", [P, 16, S], F32R)
        par = sb("par", [P, NP_])
        cst = sb("cst", [P, NC_])
        hn = sb("hn", [P, 2, S])
        sq = sb("sq", [P, 2, 2 * S])
        rs_v = sb("rs_v", [P, 2 * S])
        rs_y = sb("rs_y", [P, 2 * S])
        rs_t = sb("rs_t", [P, 2 * S])
        neg_max = sb("neg_max", [P, 4])
        z_sum = sb("z_sum", [P, 4])
        z_inv = sb("z_inv", [P, 4])
        ARENA = 16896
        arena = sb("arena", [P, ARENA])
        bank = [ctx.enter_context(nc.psum_tensor(f"bank{i}", [P, 512], F32)) for i in range(8)]
        stat = bank[7]
        DOWN0 = 3

        raw_full = [sem(f"raw_full{i}") for i in range(RING)]
        bias_full = [sem(f"bias_full{i}") for i in range(2)]
        x_loaded, consts_loaded, rpb_loaded, stored = sem("x_loaded"), sem("consts_loaded"), sem("rpb_loaded"), sem("stored")
        hi_done, lo_done, chunk_used = sem("hi_done"), sem("lo_done"), sem("chunk_used")
        x_ready = sem("x_ready")
        sq_done, sum_done, stat_read = sem("sq_done"), sem("sum_done"), sem("stat_read")
        ars_done, newton = sem("ars_done"), sem("newton")
        hn_done, hhi_done, hlo_done = sem("hn_done"), sem("hhi_done"), sem("hlo_done")
        evac_done = sem("evac_done")
        up_ready, sum_ready = sem("up_ready"), sem("sum_ready")
        lin_done, taps_done, gelu_done = sem("lin_done"), sem("taps_done"), sem("gelu_done")
        prod_done, uhi_done, ulo_done = sem("prod_done"), sem("uhi_done"), sem("ulo_done")
        score_done, biased, exp_done, scaled = sem("score_done"), sem("biased"), sem("exp_done"), sem("scaled")
        pt_done, ptc_done, pv_done, yev_done = sem("pt_done"), sem("ptc_done"), sem("pv_done"), sem("yev_done")
        rope_step, post_step, table_masked, table_step, nq_done = sem("rope_step"), sem("post_step"), sem("table_masked"), sem("table_step"), sem("nq_done")
        diag_done, pe_taps_done = sem("diag_done"), sem("pe_taps_done")
        gate_done, glu_done, pad_done, conv_step = sem("gate_done"), sem("glu_done"), sem("pad_done"), sem("conv_step")
        centred, silu_done = sem("centred"), sem("silu_done")
        rot_v, rot_p = sem("rot_v"), sem("rot_p")
        dec_v, dec_a, mask_v, mask_a, prob_done = sem("dec_v"), sem("dec_a"), sem("mask_v"), sem("mask_a"), sem("prob_done")
        ret_out, gated, flipped = sem("ret_out"), sem("gated"), sem("flipped")

        def pe_taps(m):
            return range(CW - PE_TAPS[m], CW)

        def half_bank(m):
            return bank[DOWN0 + m // 2][:, (m % 2) * S:(m % 2 + 1) * S]

        def diag_slot(m, tap):
            return sum(PE_TAPS[:m]) + tap - (CW - PE_TAPS[m])

        def cc(name, n, p0=0, p1=P):
            return cst[p0:p1, CA[name]:CA[name] + n]

        def pcol(name, i=0):
            return par[:, PA[name] + i:PA[name] + i + 1]

        def pair(view, t):
            return view[:, 2 * t:2 * t + 2, :].rearrange("p a b -> p (a b)")

        def halves(view):
            return view.rearrange("p (a b) -> p a b", a=2)

        def region(off, *dims):
            n = int(np.prod(dims))
            assert off + n <= ARENA, (off, n)
            v = arena[:, off:off + n]
            if len(dims) == 2:
                v = v.rearrange("p (a b) -> p a b", a=dims[0])
            return v

        sc_buf = region(0, 3, 512)
        pt_buf = region(1536, 2, 512)
        y_att = region(2560, 8, S)
        A0 = 4608
        qk_a = region(A0, 8, S)
        v_a = region(A0 + 2048, 2, 512)
        lat = region(A0 + 3072, 6, S)
        q_b = region(A0 + 4608, HB, S)
        k_b = region(A0 + 6656, HB, S)
        v_b = region(A0 + 8704, 2, 512)
        rope_t = region(A0 + 9728, 2, 512)
        bias_a = region(A0 + 10752, 2, 512)
        qk_n = region(A0, 16, S)
        v_n = region(A0 + 4096, 2, D)
        t_n = region(A0 + 6144, NH * 6 * GW)
        t_up = region(A0, NH * 6 * GW)
        lin = region(0, 2, 512)
        u32 = region(1024, 2, S)
        up_n = region(1536, 2, 512)
        y_post = region(2560, 8, S)
        UP = S + 2 * PADC
        u_pad = region(0, DT, UP)
        c_acc = region(DT * UP, DT, S)
        c_sg = region(DT * (UP + S), 2, S)
        DG0 = DT * (UP + S) + 2 * S
        diag = region(DG0, (ARENA - DG0) // P, P)
        q_r, k_r = region(0, 8, S), region(2048, 8, S)
        v_r, g_r = region(4096, 2, 2048), region(8192, 16, S)
        p_r, d_r, rot = region(12288, 2, 512), region(13312, 2, 512), region(14336, 4, 512)
        dec = region(16384, 8, 8)

        def o_ret(h, e):
            return (q_r if e < 2 else k_r)[:, 2 * h + e % 2, :]

        block = ctx.enter_context(nc.Block())

        @block.sync
        def _(sp):
            def load(c):
                if c >= RING:
                    sp.wait_ge(lo_done, c - RING + 1)
                sp.dma_start(raw[:, c % RING, 0:widths[c]], wstream[c, :, 0:widths[c]]).then_inc(raw_full[c % RING], 16)

            sp.dma_start(x[:, :, :], x_in.rearrange("t p s -> p t s")).then_inc(x_loaded, 16)
            load(0)
            sp.dma_start(par[:, :], params_in).then_inc(consts_loaded, 16)
            sp.dma_start(cst[:, :], consts_in).then_inc(consts_loaded, 16)
            uneven = max([c + 1 for c in range(n_chunks) if widths[c] != CH] + [RING])
            start = -(-uneven // RING)
            end = n_chunks // RING
            for c in range(1, start * RING):
                load(c)
            with sp.Fori(start, end) as i:
                for s in range(RING):
                    sp.wait_ge(lo_done, i * RING + (s - RING + 1))
                    sp.dma_start(raw[:, s, :], wstream[bass.ds(i * RING + s, 1)].rearrange("a p n -> (a p) n"))\
                      .then_inc(raw_full[s], 16)
            for c in range(end * RING, n_chunks):
                load(c)
            sp.wait_ge(x_ready, 4 * len(stages))
            sp.dma_start(out.rearrange("t p s -> p t s"), x[:, :, :]).then_inc(stored, 16)
            for s in range(RING):
                sp.wait_ge(raw_full[s], 16 * len(range(s, n_chunks, RING)))
            sp.wait_ge(stored, 16)

        @block.gpsimd
        def _(pool):
            k = Counter()

            def diagonals(j):
                for m in range(DT):
                    for tap in pe_taps(m):
                        ins = nc.gpsimd.tensor_scalar(diag[:, diag_slot(m, tap), :], cc("ident", P),
                                                      pcol("conv_dw_w_2", (8 * j + m) * CW + tap), None, ALU.mult)
                    ins.then_inc(diag_done, 1)

            def bias_table():
                for h in range(NH):
                    for half in range(2):
                        src = bass.AP(tensor=rpb_in.tensor, offset=rpb_in[h, 5 - half:6 - half, 0:1].offset,
                                      ap=[[1, GW], [P, 6], [1, GW]])
                        dst = t_up[64 * half:64 * half + 64, h * 6 * GW:(h + 1) * 6 * GW]
                        pool.dma_start(dst.rearrange("p (a b) -> p a b", a=6), src).then_inc(rpb_loaded, 16)
                pool.wait_ge(rpb_loaded, 16 * 2 * NH)
                mask = cc("nat_mask", GW).unsqueeze(1).broadcast_to([P, 8, GW])
                for n in range(12):
                    part = t_up[:, n * 512:(n + 1) * 512].rearrange("p (a b) -> p a b", b=GW)
                    nc.gpsimd.tensor_tensor(part, part, mask, ALU.add).then_inc(table_masked, 1)

            pool.wait_ge(consts_loaded, 32)
            for name in stages:
                c0 = first_chunk[name]
                if name == "mix":
                    for h in range(HA):
                        if h >= 2:
                            pool.wait_ge(biased, 2 * (h - 2) + 1)
                        pool.dma_start(bias_a[:, h % 2, :], bias_in[:, h * 512:(h + 1) * 512]).then_inc(bias_full[h % 2], 16)
                if name.startswith("conv"):
                    if c0 == 0:
                        diagonals(int(name[4:]))
                    if k["x"]:
                        pool.wait_ge(x_ready, k["x"])
                    nc.gpsimd.memset(u_pad[:, :, 0:PADC], 0.0).then_inc(pad_done, 1)
                    nc.gpsimd.memset(u_pad[:, :, PADC + S:UP], 0.0).then_inc(pad_done, 1)
                if name == "nat" and c0 == 0:
                    bias_table()
                if name == "ret":
                    for c in range(8):
                        dst = (k_r if c % 2 else q_r)[:, 2 * (c // 2):2 * (c // 2) + 2, :]
                        a, b = rot[:, 2 * (c % 2), :], rot[:, 2 * (c % 2) + 1, :]
                        pool.wait_ge(rot_v, k["rot_v"] + 2 * c + 2)
                        nc.gpsimd.tensor_tensor(dst[:, 0, :], a[:, 0:S], b[:, S:2 * S], ALU.subtract).then_inc(rot_p, 1)
                        nc.gpsimd.tensor_tensor(dst[:, 1, :], b[:, 0:S], a[:, S:2 * S], ALU.add).then_inc(rot_p, 1)
                    k["rot_v"] += 16
                after = stages[stages.index(name) + 1:][:1]
                if after and after[0].startswith("conv"):
                    if k["x"]:
                        pool.wait_ge(x_ready, k["x"])
                    diagonals(int(after[0][4:]))
                if after == ("nat",):
                    if k["x"]:
                        pool.wait_ge(x_ready, k["x"])
                    bias_table()
                k["x"] += 4

        @block.scalar
        def _(act):
            k = Counter()

            def split_hi(c):
                if c >= n_chunks:
                    return
                w = widths[c]
                act.wait_ge(raw_full[c % RING], 16 * (c // RING + 1))
                if c >= RING:
                    act.wait_ge(chunk_used, c - RING + 1)
                nc.scalar.activation(w_hi[:, c % RING, 0:w], raw[:, c % RING, 0:w], ACT.Copy).then_inc(hi_done, 1)

            def squares(sources):
                for view, width, ready, value in sources:
                    g = k["sq"]
                    act.wait_ge(ready, value)
                    if g >= 2:
                        act.wait_ge(sum_done, k["sum"] - 1)
                    nc.scalar.activation(sq[:, g % 2, 0:width], view, ACT.Square).then_inc(sq_done, 1)
                    k["sq"] += 1
                    k["sum"] += 1

            def inv_sqrt(width=S):
                k["stat"] += 1
                act.wait_ge(stat_read, k["stat"])
                nc.scalar.activation(rs_y[:, 0:width], rs_v[:, 0:width], ACT.Abs_reciprocal_sqrt).then_inc(ars_done, 1)

            def split_h(tiles, silu=None):
                for i, t in enumerate(tiles):
                    act.wait_ge(hn_done, k["hn"] + 1)
                    h = hn[:, k["slot"] % 2, :]
                    if silu:
                        nc.scalar.activation(h, h, ACT.Silu, bias=silu(i)).then_inc(silu_done, 1)
                        k["silu"] += 1
                        act.wait_ge(silu_done, k["silu"])
                    nc.scalar.activation(h_hi[:, t, :], h, ACT.Copy).then_inc(hhi_done, 1)
                    k["hn"] += 1
                    k["slot"] += 1

            def evac(c, dst, src, func=ACT.Copy):
                act.wait_ge(chunk_used, c + 1)
                nc.scalar.activation(dst, src, func).then_inc(evac_done, 1)
                k["evac"] += 1

            def x_pairs(a, b):
                return [(pair(x, t), 512) + ((x_ready, k["x"] - 3 + t) if k["x"] else (x_loaded, 16)) for t in range(a, b)]

            def prenorm():
                squares(x_pairs(0, 4))
                inv_sqrt()
                split_h(range(DT))

            def y_evac(p_):
                act.wait_ge(pv_done, 2 * p_ + 2)
                nc.scalar.activation(y_att[:, p_ % 8, :], bank[4 + p_ % 2][:, 0:S], ACT.Copy).then_inc(yev_done, 1)

            def attention():
                g0 = k["heads"]
                for g in range(g0, g0 + 17):
                    if g < g0 + 16:
                        act.wait_ge(biased, 2 * g + 2)
                        if g >= 2:
                            act.wait_ge(scaled, 3 * (g - 2) + 1)
                        for j in range(2):
                            i = 2 * (g % 2) + j
                            view = sc_buf[:, g % 3, j * S:(j + 1) * S]
                            nc.scalar.activation(view, view, ACT.Exp, bias=neg_max[:, i:i + 1],
                                                 accum_out=z_sum[:, i:i + 1]).then_inc(exp_done, 1)
                    if g > g0:
                        act.wait_ge(pt_done, g)
                        if g - 1 >= 2:
                            act.wait_ge(pv_done, g - 2)
                        nc.scalar.activation(pt_buf[:, (g - 1) % 2, :], bank[2 + (g - 1) % 2][:, :], ACT.Copy)\
                                 .then_inc(ptc_done, 1)
                    if g >= g0 + 3 and (g - g0) % 2 == 1:
                        y_evac((g - 3) // 2)
                y_evac((g0 + 14) // 2)
                k["heads"] += 16

            def ffn(index, c0):
                T0 = k["ffn"] * FT
                pb = PA["ffn_dw"] + index * FT * 8

                def centre(t, a):
                    act.wait_ge(up_ready, t + (T0 + 1))
                    if not isinstance(t, int) or t >= 2:
                        act.wait_ge(prod_done, t + (T0 - 1))
                    for w in range(2):
                        def tap(n):
                            return par[:, bass.ds(t * 8 + (pb + 4 * w + n), 1)]
                        nc.scalar.activation(lin[:, a, w * S:(w + 1) * S], up_n[:, a, w * S:(w + 1) * S],
                                             ACT.Identity, bias=tap(3), scale=tap(1)).then_inc(lin_done, 1)

                def gelu(t, a):
                    act.wait_ge(taps_done, t * 4 + (4 * T0 + 3))
                    nc.scalar.activation(lin[:, a, 0:S], lin[:, a, 0:S], ACT.Gelu_apprx_tanh).then_inc(gelu_done, 1)

                def loop_split(i, a):
                    c = c0 + 1 + a
                    act.wait_ge(raw_full[c % RING], i * 16 + 16 * (c // RING + 1))
                    act.wait_ge(chunk_used, i * 3 + (c - RING + 1))
                    nc.scalar.activation(w_hi[:, c % RING, :], raw[:, c % RING, :], ACT.Copy).then_inc(hi_done, 1)

                split_h(range(DT))
                squares(x_pairs(0, 2))
                split_hi(c0 + 2)
                squares(x_pairs(2, 4))
                inv_sqrt()
                for a in range(2):
                    centre(a, a)
                    if a == 0:
                        split_hi(c0 + 3)
                    gelu(a, a)
                with act.Fori(1, FT // 2) as i:
                    loop_split(i, 0)
                    for a in range(2):
                        centre(i * 2 + a, a)
                        loop_split(i, 1 + a)
                        gelu(i * 2 + a, a)
                split_hi(c0 + 34)
                k["ffn"] += 1

            act.wait_ge(consts_loaded, 32)
            split_hi(0)
            split_hi(1)
            for name in stages:
                c0 = first_chunk[name]
                if name == "nat":
                    def table_part(n):
                        act.wait_ge(flipped, n + 1)
                        nc.scalar.activation(t_n[:, n * 512:(n + 1) * 512], bank[DOWN0 + n % 4][:, :], ACT.Copy)\
                                 .then_inc(table_step, 1)
                if not name.startswith("ffn"):
                    prenorm()
                if name == "mix":
                    for c in range(9):
                        split_hi(c0 + c + 2)
                        src = bank[(c0 + c) % 3][:, :]
                        if c < 4:
                            evac(c0 + c, pair(qk_a, c), src)
                        elif c < 6:
                            evac(c0 + c, v_a[:, :, (c - 4) * S:(c - 3) * S], halves(src))
                        else:
                            evac(c0 + c, pair(lat, c - 6), src)
                    for lo, hi in ((0, 3), (3, 5)):
                        squares([(lat[:, t, :], S, evac_done, k["evac"]) for t in range(lo, hi)])
                        inv_sqrt()
                        split_h(range(8 + lo, 8 + hi))
                    for c in range(9, 19):
                        split_hi(c0 + c + 2)
                        src = bank[(c0 + c) % 3]
                        if c < 17:
                            dst = q_b if c < 13 else k_b
                            j = (c - 9) % 4
                            evac(c0 + c, dst[0:64, 2 * j:2 * j + 2, :], halves(src[0:64, :]))
                        else:
                            evac(c0 + c, v_b[:, :, (c - 17) * S:(c - 16) * S], halves(src[:, :]))
                    attention()
                    for half in range(2):
                        p_ = k["heads"] // 2 - 8
                        squares([(y_att[:, t, :], S, yev_done, p_ + t + 1) for t in range(4 * half, 4 * half + 4)])
                        inv_sqrt()
                        split_h(range(4 * half, 4 * half + 4))
                    for c in range(19, 23):
                        split_hi(c0 + c + 2)
                        evac(c0 + c, pair(qk_a, c - 19), bank[(c0 + c) % 3][:, :])
                        squares([(pair(qk_a, c - 19), 512, evac_done, k["evac"])])
                    inv_sqrt()
                elif name.startswith("ffn"):
                    ffn(int(name[3:]), c0)
                    if name == "ffn0":
                        for c in range(4):
                            evac(c0 + 32, pair(y_post, c), bank[DOWN0 + c][:, :])
                            squares([(pair(y_post, c), 512, evac_done, k["evac"])])
                        inv_sqrt()
                elif name.startswith("conv"):
                    j = int(name[4:])
                    for c in range(8):
                        split_hi(c0 + c + 2)
                        act.wait_ge(chunk_used, c0 + c + 1)
                        if k["gate"] >= 2:
                            act.wait_ge(glu_done, k["gate"] - 1)
                        nc.scalar.activation(c_sg[:, c % 2, :], bank[(c0 + c) % 3][:, S:2 * S], ACT.Sigmoid,
                                             bias=pcol("conv_b_in_2", 16 * j + 8 + c)).then_inc(gate_done, 1)
                        k["gate"] += 1
                    k["sum"] += 8
                    k["stat"] += 1
                    k["centred"] += 8
                    squares([(pair(c_acc, t), 512, centred, k["centred"] - 8 + 2 * t + 2) for t in range(4)])
                    inv_sqrt()
                    split_h(range(DT), silu=lambda t: pcol("conv_ln_b_2", 8 * j + t))
                    for c in range(8, 12):
                        split_hi(c0 + c + 2)
                elif name == "nat":
                    for n in range(4):
                        table_part(n)
                    for c in range(12):
                        split_hi(c0 + c + 2)
                        src = bank[(c0 + c) % 3][:, :]
                        if c < 8:
                            evac(c0 + c, pair(qk_n, c), src)
                            squares([(pair(qk_n, c), 512, evac_done, k["evac"])])
                            inv_sqrt(512)
                            table_part(4 + c)
                        else:
                            evac(c0 + c, v_n[:, :, (c - 8) * S:(c - 7) * S], halves(src))
                    attention()
                    for t in range(8):
                        act.wait_ge(yev_done, k["heads"] // 2 - 8 + t + 1)
                        nc.scalar.activation(h_hi[:, t, :], y_att[:, t, :], ACT.Copy).then_inc(hhi_done, 1)
                    for c in range(12, 16):
                        split_hi(c0 + c + 2)
                elif name == "ret":
                    nc.scalar.activation(dec[:, 0, :], par[:, PA["ret_log2_inv_decay_2"]:PA["ret_log2_inv_decay_2"] + 8],
                                         ACT.Exp, scale=-math.log(2.0)).then_inc(dec_a, 1)
                    act.wait_ge(dec_v, 1)
                    nc.scalar.activation(dec[:, 2, :], dec[:, 1, :], ACT.Ln).then_inc(dec_a, 1)
                    for c in range(8):
                        split_hi(c0 + c + 2)
                    for c in range(8, 16):
                        split_hi(c0 + c + 2)
                        evac(c0 + c, v_r[:, :, (c - 8) * S:(c - 7) * S], halves(bank[(c0 + c) % 3][:, :]))
                    for c in range(16, 24):
                        split_hi(c0 + c + 2)
                        evac(c0 + c, pair(g_r, c - 16), bank[(c0 + c) % 3][:, :], ACT.Silu)
                    for h in range(RH):
                        act.wait_ge(mask_v, 2 * h + 2)
                        nc.scalar.activation(d_r[:, h % 2, :], d_r[:, h % 2, :], ACT.Exp).then_inc(mask_a, 1)
                        for e in range(2):
                            act.wait_ge(ret_out, 2 * h + e + 1)
                            nc.scalar.activation((q_r, k_r)[e][:, 2 * h:2 * h + 2, :],
                                                 halves(bank[3 + 2 * (h % 2) + e][:, :]), ACT.Copy).then_inc(evac_done, 1)
                            k["evac"] += 1
                    for h in range(RH):
                        k["sum"] += 2
                        k["stat"] += 1
                        k["centred"] += 2
                        squares([((q_r, k_r)[e][:, 2 * h:2 * h + 2, :].rearrange("p a b -> p (a b)"), 512, centred,
                                  k["centred"] - 1 + e) for e in range(2)])
                        inv_sqrt()
                        split_h(range(4 * h, 4 * h + 4))
                    for c in range(24, 32):
                        split_hi(c0 + c + 2)
                k["x"] += 4

        @block.vector
        def _(dve):
            k = Counter()
            slot_free = [0, 0]

            def split_lo(c):
                if c >= n_chunks:
                    return
                w, s = widths[c], c % RING
                dve.wait_ge(hi_done, c + 1)
                nc.vector.tensor_tensor(w_lo[:, s, 0:w], raw[:, s, 0:w], w_hi[:, s, 0:w].bitcast(F32), ALU.subtract)\
                         .then_inc(lo_done, 1)

            def root(n_sums, scale, width=S):
                k["sum"] += n_sums
                k["stat"] += 1
                v, y, t = rs_v[:, 0:width], rs_y[:, 0:width], rs_t[:, 0:width]
                dve.wait_ge(sum_done, k["sum"])
                if k["newton"]:
                    dve.wait_ge(newton, k["newton"])
                nc.vector.tensor_scalar(v, stat[:, 0:width], scale, EPS, ALU.mult, ALU.add).then_inc(stat_read, 1)
                k["ars"] += 1
                dve.wait_ge(ars_done, k["ars"])
                nc.vector.tensor_tensor(t, y, y, ALU.mult).then_inc(newton, 1)
                dve.wait_ge(newton, k["newton"] + 1)
                nc.vector.scalar_tensor_tensor(t, t, -0.5, v, ALU.mult, ALU.mult).then_inc(newton, 1)
                dve.wait_ge(newton, k["newton"] + 2)
                nc.vector.scalar_tensor_tensor(y, t, 1.5, y, ALU.add, ALU.mult).then_inc(newton, 1)
                k["newton"] += 3
                dve.wait_ge(newton, k["newton"])

            def normalize(sources, times=None, by_root=True):
                def lo(i):
                    slot, n_hhi, n_lo, t = pending[i]
                    dve.wait_ge(hhi_done, n_hhi)
                    nc.vector.tensor_tensor(h_lo[:, t, :], hn[:, slot, :], h_hi[:, t, :].bitcast(F32), ALU.subtract)\
                             .then_inc(hlo_done, 1)

                pending = []
                for i, (view, gain, t) in enumerate(sources):
                    slot = k["slot"] % 2
                    if slot_free[slot]:
                        dve.wait_ge(hlo_done, slot_free[slot])
                    if by_root:
                        first = nc.vector.scalar_tensor_tensor(hn[:, slot, :], view, gain, rs_y[:, 0:S], ALU.mult, ALU.mult)
                    else:
                        first = nc.vector.tensor_scalar(hn[:, slot, :], view, gain, None, ALU.mult)
                    if times:
                        first.then_inc(gated, 1)
                        k["gated"] += 1
                        dve.wait_ge(gated, k["gated"])
                        nc.vector.tensor_tensor(hn[:, slot, :], hn[:, slot, :], times(i), ALU.mult).then_inc(hn_done, 1)
                    else:
                        first.then_inc(hn_done, 1)
                    k["hhi"] += 1
                    k["hlo"] += 1
                    k["slot"] += 1
                    slot_free[slot] = k["hlo"]
                    pending.append((slot, k["hhi"], k["hlo"], t))
                    if i >= 1:
                        lo(i - 1)
                lo(len(pending) - 1)

            def prenorm(gain):
                root(4, 1.0 / D)
                normalize([(x[:, t, :], gain(t), t) for t in range(DT)])

            def residual(c, t, src):
                dve.wait_ge(chunk_used, c + 1)
                nc.vector.tensor_tensor(pair(x, t), pair(x, t), src, ALU.add).then_inc(x_ready, 1)

            def post(y, gain):
                root(4, 1.0 / D)
                for t in range(DT + 1):
                    if t < DT:
                        nc.vector.scalar_tensor_tensor(y[:, t, :], y[:, t, :], gain(t), rs_y[:, 0:S], ALU.mult, ALU.mult)\
                                 .then_inc(post_step, 1)
                        k["post"] += 1
                    if t >= 1:
                        dve.wait_ge(post_step, k["post"] - (1 if t < DT else 0))
                        ins = nc.vector.tensor_tensor(x[:, t - 1, :], x[:, t - 1, :], y[:, t - 1, :], ALU.add)
                        if t % 2 == 0:
                            ins.then_inc(x_ready, 1)

            def attention(scale_of, bias_of):
                g0 = k["heads"]
                for g in range(g0, g0 + 17):
                    if g < g0 + 16:
                        h = g - g0
                        dve.wait_ge(score_done, g + 1)
                        if g >= 3:
                            dve.wait_ge(pt_done, g - 2)
                        s = sc_buf[:, g % 3, :]
                        bias, wait = bias_of(h)
                        if wait:
                            dve.wait_ge(*wait)
                        if bias is None:
                            nc.vector.tensor_scalar(s, bank[g % 2][:, :], scale_of(h), None, ALU.mult).then_inc(biased, 1)
                        elif len(bias) == 1:
                            nc.vector.scalar_tensor_tensor(s, bank[g % 2][:, :], scale_of(h), bias[0], ALU.mult, ALU.add)\
                                     .then_inc(biased, 1)
                        else:
                            for j in range(2):
                                ins = nc.vector.scalar_tensor_tensor(s[:, j * S:(j + 1) * S], bank[g % 2][:, j * S:(j + 1) * S],
                                                                     scale_of(h), bias[j], ALU.mult, ALU.add)
                            ins.then_inc(biased, 1)
                        dve.wait_ge(biased, 2 * g + 1)
                        if g >= 2:
                            dve.wait_ge(exp_done, 2 * (g - 2) + 2)
                        nc.vector.tensor_reduce(neg_max[:, 2 * (g % 2):2 * (g % 2) + 2], halves(s), AX.X, ALU.max, negate=True)\
                                 .then_inc(biased, 1)
                    if g > g0:
                        q = g - 1
                        zi = z_inv[:, 2 * (q % 2):2 * (q % 2) + 2]
                        dve.wait_ge(exp_done, 2 * q + 2)
                        nc.vector.reciprocal(zi, z_sum[:, 2 * (q % 2):2 * (q % 2) + 2]).then_inc(scaled, 1)
                        dve.wait_ge(scaled, 3 * q + 1)
                        for j in range(2):
                            s = sc_buf[:, q % 3, j * S:(j + 1) * S]
                            nc.vector.tensor_scalar(s, s, zi[:, j:j + 1], None, ALU.mult).then_inc(scaled, 1)
                k["heads"] += 16

            def ffn(index, c0, gain):
                T0 = k["ffn"] * FT
                pb = PA["ffn_dw"] + index * FT * 8

                def up_norm(t, a, bank_, used):
                    dve.wait_ge(chunk_used, used)
                    if not isinstance(t, int) or t >= 2:
                        dve.wait_ge(taps_done, t * 4 + (4 * T0 - 4))
                    nc.vector.tensor_tensor(halves(up_n[:, a, :]), halves(bank[bank_][:, :]),
                                            rs_y[:, 0:S].unsqueeze(1).broadcast_to([P, 2, S]), ALU.mult).then_inc(up_ready, 1)

                def taps(t, a):
                    for n in range(4):
                        w = n % 2
                        src, dst = up_n[:, a, w * S:(w + 1) * S], lin[:, a, w * S:(w + 1) * S]
                        if n < 2:
                            dve.wait_ge(lin_done, t * 2 + (2 * T0 + 2))
                            o, i_, tap = dst[:, 1:S], src[:, 0:S - 1], 0
                        else:
                            dve.wait_ge(taps_done, t * 4 + (4 * T0 + n - 1))
                            o, i_, tap = dst[:, 0:S - 1], src[:, 1:S], 2
                        nc.vector.scalar_tensor_tensor(o, i_, par[:, bass.ds(t * 8 + (pb + 4 * w + tap), 1)], o,
                                                       ALU.mult, ALU.add).then_inc(taps_done, 1)

                def gated_value(t, a):
                    dve.wait_ge(gelu_done, t + (T0 + 1))
                    dve.wait_ge(taps_done, t * 4 + (4 * T0 + 4))
                    if not isinstance(t, int) or t >= 2:
                        dve.wait_ge(ulo_done, t + (T0 - 1))
                    nc.vector.tensor_tensor(u32[:, a, :], lin[:, a, 0:S], lin[:, a, S:2 * S], ALU.mult).then_inc(prod_done, 1)

                def parts(t, a, d_used):
                    dve.wait_ge(prod_done, t + (T0 + 1))
                    dve.wait_ge(chunk_used, d_used)
                    nc.vector.tensor_copy(h_hi[:, 8 + a, :], u32[:, a, :]).then_inc(uhi_done, 1)
                    dve.wait_ge(uhi_done, t + (T0 + 1))
                    nc.vector.tensor_tensor(h_lo[:, 8 + a, :], u32[:, a, :], h_hi[:, 8 + a, :].bitcast(F32), ALU.subtract)\
                             .then_inc(ulo_done, 1)

                def loop_split(i, a):
                    c = c0 + 1 + a
                    dve.wait_ge(hi_done, i * 3 + (c + 1))
                    nc.vector.tensor_tensor(w_lo[:, c % RING, :], raw[:, c % RING, :], w_hi[:, c % RING, :].bitcast(F32),
                                            ALU.subtract).then_inc(lo_done, 1)

                normalize([(x[:, t, :], gain(t), t) for t in range(DT)], by_root=False)
                split_lo(c0 + 2)
                root(4, 1.0 / D)
                up_norm(0, 0, c0 % 3, c0 + 1)
                taps(0, 0)
                up_norm(1, 1, (c0 + 1) % 3, c0 + 2)
                gated_value(0, 0)
                taps(1, 1)
                with dve.Fori(1, FT // 2) as i:
                    used = i * 3 + (c0 - 1)
                    parts(i * 2 + (-2), 0, used)
                    loop_split(i, -1)
                    loop_split(i, 0)
                    up_norm(i * 2, 0, (c0 + 2) % 3, i * 3 + c0)
                    gated_value(i * 2 + (-1), 1)
                    parts(i * 2 + (-1), 1, used)
                    taps(i * 2, 0)
                    loop_split(i, 1)
                    up_norm(i * 2 + 1, 1, (c0 + 3) % 3, i * 3 + (c0 + 1))
                    gated_value(i * 2, 0)
                    taps(i * 2 + 1, 1)
                parts(FT - 2, 0, c0 + 3 * (FT // 2) - 1)
                gated_value(FT - 1, 1)
                parts(FT - 1, 1, c0 + 3 * (FT // 2) - 1)
                split_lo(c0 + 33)
                split_lo(c0 + 34)
                k["ffn"] += 1

            dve.wait_ge(consts_loaded, 32)
            dve.wait_ge(x_loaded, 16)
            split_lo(0)
            split_lo(1)
            for name in stages:
                c0 = first_chunk[name]
                if name == "mix":
                    prenorm(lambda t: pcol("norm_mix_pre", t))
                    for c in range(9):
                        split_lo(c0 + c + 2)
                        k["evac"] += 1
                    for lo, hi, gain, n in ((0, 3, "q_lat_norm", QL), (3, 5, "kv_lat_norm", KL)):
                        root(hi - lo, 1.0 / n)
                        normalize([(lat[:, t, :], pcol(gain, t - lo), 8 + t) for t in range(lo, hi)])
                    cos, sin = cc("rope_cos", S, 64, 96), cc("rope_sin", S, 96, 128)
                    cos2 = cos.unsqueeze(1).broadcast_to([32, 2, S])
                    sin2 = sin.unsqueeze(1).broadcast_to([32, 2, S])
                    for c in range(9, 19):
                        split_lo(c0 + c + 2)
                        k["evac"] += 1
                        if c < 13:
                            src = bank[(c0 + c) % 3]
                            dve.wait_ge(chunk_used, c0 + c + 1)
                            if c > 9:
                                dve.wait_ge(rope_step, k["rope"])
                            nc.vector.tensor_tensor(halves(rope_t[64:96, 0, :]), halves(src[64:96, :]), cos2, ALU.mult)\
                                     .then_inc(rope_step, 1)
                            nc.vector.tensor_tensor(halves(rope_t[64:96, 1, :]), halves(src[96:128, :]), sin2, ALU.mult)\
                                     .then_inc(rope_step, 1)
                            dve.wait_ge(rope_step, k["rope"] + 2)
                            j = c - 9
                            nc.vector.tensor_tensor(q_b[64:96, 2 * j:2 * j + 2, :], halves(rope_t[64:96, 0, :]),
                                                    halves(rope_t[64:96, 1, :]), ALU.add).then_inc(rope_step, 1)
                            k["rope"] += 3
                    dve.wait_ge(rope_step, k["rope"])
                    nc.vector.tensor_tensor(rope_t[64:96, 0, 0:S], lat[64:96, 5, :], cos, ALU.mult).then_inc(rope_step, 1)
                    nc.vector.tensor_tensor(rope_t[64:96, 1, 0:S], lat[96:128, 5, :], sin, ALU.mult).then_inc(rope_step, 1)
                    dve.wait_ge(rope_step, k["rope"] + 2)
                    nc.vector.tensor_tensor(k_b[64:96, :, :], rope_t[64:96, 0, 0:S].unsqueeze(1).broadcast_to([32, HB, S]),
                                            rope_t[64:96, 1, 0:S].unsqueeze(1).broadcast_to([32, HB, S]), ALU.add)\
                             .then_inc(rope_step, 1)
                    k["rope"] += 3
                    attention(lambda h: HDA ** -0.5 if h < HA else (NOPE + ROPE) ** -0.5,
                              lambda h: ([bias_a[:, h % 2, :]], (bias_full[h % 2], 16 * (h // 2 + 1))) if h < HA else (None, None))
                    for half, gain in enumerate(("out_norm_a", "out_norm_b")):
                        root(4, 1.0 / 512)
                        normalize([(y_att[:, t, :], pcol(gain, t % 4), t) for t in range(4 * half, 4 * half + 4)])
                    for c in range(19, 23):
                        split_lo(c0 + c + 2)
                    post(qk_a, lambda t: pcol("norm_mix_post", t))
                elif name.startswith("ffn"):
                    n = int(name[3:])
                    ffn(n, c0, (lambda t: pcol("norm_ffn_pre", t)) if n == 0 else (lambda t: pcol("norm2_g_2", 8 * (n - 1) + t)))
                    if n == 0:
                        post(y_post, lambda t: pcol("norm_ffn_post", t))
                    else:
                        for t in range(4):
                            if t < 3:
                                dve.wait_ge(sum_ready, 3 * (k["ffn"] - 1) + t + 1)
                            else:
                                dve.wait_ge(chunk_used, c0 + 33)
                            nc.vector.tensor_tensor(pair(x, t), pair(x, t), bank[DOWN0 + t][:, :], ALU.add).then_inc(x_ready, 1)
                elif name.startswith("conv"):
                    j = int(name[4:])
                    layer = 3 * j
                    prenorm(lambda t: pcol("norm1_g_2", 8 * layer + t))
                    last_tap = {}
                    k["pad"] += 2
                    dve.wait_ge(pad_done, k["pad"])
                    for c in range(8):
                        split_lo(c0 + c + 2)
                        k["gate"] += 1
                        dve.wait_ge(gate_done, k["gate"])
                        nc.vector.scalar_tensor_tensor(u_pad[:, c, PADC:PADC + S], bank[(c0 + c) % 3][:, 0:S],
                                                       pcol("conv_b_in_2", 16 * j + c), c_sg[:, c % 2, :], ALU.add, ALU.mult)\
                                 .then_inc(glu_done, 1)
                        k["glu"] += 1
                        if c % 2 == 1:
                            dve.wait_ge(glu_done, k["glu"])
                            for tap in range(max(CW - PE_TAPS[m] for m in (c - 1, c))):
                                for m in (c - 1, c):
                                    if tap >= CW - PE_TAPS[m]:
                                        continue
                                    wcol = pcol("conv_dw_w_2", (8 * j + m) * CW + tap)
                                    src = u_pad[:, m, tap:tap + S]
                                    if tap == 0:
                                        nc.vector.tensor_scalar(c_acc[:, m, :], src, wcol, pcol("conv_dw_b_2", 8 * j + m),
                                                                ALU.mult, ALU.add).then_inc(conv_step, 1)
                                    else:
                                        dve.wait_ge(conv_step, last_tap[m])
                                        nc.vector.scalar_tensor_tensor(c_acc[:, m, :], src, wcol, c_acc[:, m, :],
                                                                       ALU.mult, ALU.add).then_inc(conv_step, 1)
                                    k["conv"] += 1
                                    last_tap[m] = k["conv"]
                            k["pairs"] += 1
                            dve.wait_ge(pe_taps_done, k["pairs"])
                            for m in (c - 1, c):
                                dve.wait_ge(conv_step, last_tap[m])
                                nc.vector.tensor_tensor(c_acc[:, m, :], c_acc[:, m, :], half_bank(m), ALU.add).then_inc(conv_step, 1)
                                k["conv"] += 1
                    k["sum"] += 8
                    k["stat"] += 1
                    dve.wait_ge(sum_done, k["sum"])
                    nc.vector.tensor_scalar(rs_t[:, 0:S], stat[:, 0:S], 1.0 / D, None, ALU.mult).then_inc(stat_read, 1)
                    dve.wait_ge(stat_read, k["stat"])
                    for m in range(8):
                        nc.vector.tensor_tensor(c_acc[:, m, :], c_acc[:, m, :], rs_t[:, 0:S], ALU.subtract).then_inc(centred, 1)
                    root(4, 1.0 / D)
                    normalize([(c_acc[:, t, :], pcol("conv_ln_g_2", 8 * j + t), t) for t in range(DT)])
                    for c in range(8, 12):
                        split_lo(c0 + c + 2)
                        residual(c0 + c, c - 8, bank[(c0 + c) % 3][:, :])
                elif name == "nat":
                    prenorm(lambda t: pcol("norm1_g_2", 8 + t))
                    for c in range(12):
                        split_lo(c0 + c + 2)
                        k["evac"] += 1
                        if c < 8:
                            root(1, 1.0 / NHD, 512)
                            gain = pcol("nat_q_norm_g_2" if c < 4 else "nat_k_norm_g_2")
                            nc.vector.scalar_tensor_tensor(pair(qk_n, c), pair(qk_n, c), gain, rs_y[:, :], ALU.mult, ALU.mult)\
                                     .then_inc(nq_done, 1)
                    dve.wait_ge(table_step, 12)
                    attention(lambda h: NHD ** -0.5,
                              lambda h: ([t_n[:, (6 * h + 2 - 2 * j) * GW:(6 * h + 6 - 2 * j) * GW] for j in range(2)], None))
                    for t in range(8):
                        k["hhi"] += 1
                        k["hlo"] += 1
                        dve.wait_ge(hhi_done, k["hhi"])
                        nc.vector.tensor_tensor(h_lo[:, t, :], y_att[:, t, :], h_hi[:, t, :].bitcast(F32), ALU.subtract)\
                                 .then_inc(hlo_done, 1)
                    for c in range(12, 16):
                        split_lo(c0 + c + 2)
                        residual(c0 + c, c - 12, bank[(c0 + c) % 3][:, :])
                elif name == "ret":
                    prenorm(lambda t: pcol("norm1_g_2", 16 + t))
                    P_, W_, L_, D_, R_, E_, M_, G_ = (dec[:, n, :] for n in range(8))
                    dve.wait_ge(dec_a, 1)
                    nc.vector.tensor_scalar(W_, P_, -1.0, 1.0, ALU.mult, ALU.add).then_inc(dec_v, 1)
                    dve.wait_ge(dec_v, 1)
                    nc.vector.tensor_scalar(D_, W_, -1.0, 1.0, ALU.mult, ALU.add).then_inc(dec_v, 1)
                    dve.wait_ge(dec_v, 2)
                    nc.vector.tensor_scalar(D_, D_, 1e-30, None, ALU.max).then_inc(dec_v, 1)
                    dve.wait_ge(dec_v, 3)
                    nc.vector.reciprocal(R_, D_).then_inc(dec_v, 1)
                    nc.vector.tensor_scalar(E_, W_, 1.0, None, ALU.is_equal).then_inc(dec_v, 1)
                    dve.wait_ge(dec_v, 5)
                    nc.vector.tensor_tensor(E_, E_, P_, ALU.mult).then_inc(dec_v, 1)
                    dve.wait_ge(dec_a, 2)
                    nc.vector.tensor_tensor(M_, L_, P_, ALU.mult).then_inc(dec_v, 1)
                    dve.wait_ge(dec_v, 7)
                    nc.vector.tensor_tensor(M_, M_, R_, ALU.mult).then_inc(dec_v, 1)
                    dve.wait_ge(dec_v, 8)
                    nc.vector.tensor_tensor(G_, M_, E_, ALU.subtract).then_inc(dec_v, 1)
                    cos2 = cc("rot_cos", S).unsqueeze(1).broadcast_to([P, 2, S])
                    sin2 = cc("rot_sin", S).unsqueeze(1).broadcast_to([P, 2, S])
                    for c in range(8):
                        split_lo(c0 + c + 2)
                        dve.wait_ge(chunk_used, c0 + c + 1)
                        if c >= 2:
                            dve.wait_ge(rot_p, 2 * (c - 2) + 2)
                        src = halves(bank[(c0 + c) % 3][:, :])
                        nc.vector.tensor_tensor(halves(rot[:, 2 * (c % 2), :]), src, cos2, ALU.mult).then_inc(rot_v, 1)
                        nc.vector.tensor_tensor(halves(rot[:, 2 * (c % 2) + 1, :]), src, sin2, ALU.mult).then_inc(rot_v, 1)
                    for c in range(8, 24):
                        split_lo(c0 + c + 2)
                        k["evac"] += 1
                    dve.wait_ge(dec_v, 9)
                    for h in range(RH):
                        d = d_r[:, h % 2, :]
                        if h >= 2:
                            dve.wait_ge(prob_done, h - 1)
                        nc.vector.tensor_scalar(d, cc("fwd", 512), G_[:, h:h + 1], None, ALU.mult).then_inc(mask_v, 1)
                        dve.wait_ge(mask_v, 2 * h + 1)
                        nc.vector.scalar_tensor_tensor(d, cc("bwd", 512), G_[:, 4 + h:5 + h], d, ALU.mult, ALU.add)\
                                 .then_inc(mask_v, 1)
                        dve.wait_ge(mask_a, h + 1)
                        dve.wait_ge(score_done, k["heads"] + h + 1)
                        if h >= 2:
                            dve.wait_ge(ret_out, 2 * (h - 2) + 2)
                        nc.vector.scalar_tensor_tensor(p_r[:, h % 2, :], bank[h % 2][:, :], RKD ** -0.5, d, ALU.mult, ALU.mult)\
                                 .then_inc(prob_done, 1)
                    k["heads"] += 4
                    for h in range(RH):
                        k["sum"] += 2
                        k["stat"] += 1
                        dve.wait_ge(sum_done, k["sum"])
                        nc.vector.tensor_scalar(rs_t[:, 0:S], stat[:, 0:S], 1.0 / RVD, None, ALU.mult).then_inc(stat_read, 1)
                        dve.wait_ge(stat_read, k["stat"])
                        for e in range(2):
                            o = (q_r, k_r)[e][:, 2 * h:2 * h + 2, :]
                            nc.vector.tensor_tensor(o, o, rs_t[:, 0:S].unsqueeze(1).broadcast_to([P, 2, S]), ALU.subtract)\
                                     .then_inc(centred, 1)
                        root(2, 1.0 / RVD)
                        normalize([(o_ret(h, e), pcol("ret_gn_g_2", 4 * h + e), 4 * h + e) for e in range(4)],
                                  times=lambda i, h=h: g_r[:, 4 * h + i, :])
                    for c in range(24, 32):
                        split_lo(c0 + c + 2)
                        dve.wait_ge(chunk_used, c0 + c + 1)
                        t = c - 24
                        ins = nc.vector.tensor_tensor(x[:, t, :], x[:, t, :], bank[(c0 + c) % 3][:, 0:S], ALU.add)
                        if t % 2:
                            ins.then_inc(x_ready, 1)

        @block.tensor
        def _(pe):
            k = Counter()
            ones, half_ones, ident = cc("ones", P), cc("half_ones", P), cc("ident", P)

            def product(dst, w_parts, x_parts, start, stop, **kw):
                nc.tensor.matmul(dst, w_parts[0], x_parts[0], start=start, stop=False, **kw)
                nc.tensor.matmul(dst, w_parts[1], x_parts[0], start=False, stop=False, **kw)
                return nc.tensor.matmul(dst, w_parts[0], x_parts[1], start=False, stop=stop, **kw)

            def weights(c, at, n=P):
                s = c % RING
                return w_hi[:, s, at:at + n], w_lo[:, s, at:at + n]

            def h_parts(t, a=0, n=S):
                return h_hi[:, t, a:a + n], h_lo[:, t, a:a + n]

            def feature_chunk(c, h0=0, n_k=8, n_m=2, wait_h=None, free=None):
                if free:
                    pe.wait_ge(*free)
                pe.wait_ge(lo_done, c + 1)
                for m in range(n_m):
                    for t in range(n_k):
                        if wait_h is not None and m == 0:
                            pe.wait_ge(hlo_done, wait_h + t + 1)
                        last = product(bank[c % 3][:, m * S:(m + 1) * S], weights(c, (m * n_k + t) * P), h_parts(h0 + t),
                                       t == 0, t == n_k - 1)
                last.then_inc(chunk_used, 1)

            def token_chunk(c, h0=0, n_k=8, free=None):
                if free:
                    pe.wait_ge(*free)
                pe.wait_ge(lo_done, c + 1)
                for j in range(2):
                    for t in range(n_k):
                        dst = bank[c % 3][:, j * S:(j + 1) * S]
                        a, b = h_parts(h0 + t, j * P, P)
                        w = weights(c, t * S, S)
                        nc.tensor.matmul(dst, a, w[0], start=t == 0, stop=False)
                        nc.tensor.matmul(dst, a, w[1], start=False, stop=False)
                        last = nc.tensor.matmul(dst, b, w[0], start=False, stop=t == n_k - 1)
                last.then_inc(chunk_used, 1)

            def sums(sources, matrix=None, width=S, start=True, stop=True):
                if k["stat"] and start:
                    pe.wait_ge(stat_read, k["stat"])
                matrix = ones if matrix is None else matrix
                n = len(sources)
                for i, (views, ready, value) in enumerate(sources):
                    pe.wait_ge(ready, value)
                    for v, view in enumerate(views):
                        last = nc.tensor.matmul(stat[:, 0:width], matrix, view, start=start and i == 0 and v == 0,
                                                stop=stop and i == n - 1 and v == len(views) - 1)
                    last.then_inc(sum_done, 1)
                k["stat"] += stop

            def sum_squares(widths_, matrix=None, start=True, stop=True):
                for_sum = []
                for w in widths_:
                    g = k["sq"]
                    k["sq"] += 1
                    if matrix is None:
                        views = [sq[:, g % 2, a:a + S] for a in range(0, w, S)]
                    else:
                        views = [sq[:, g % 2, 0:w]]
                    for_sum.append((views, sq_done, g + 1))
                sums(for_sum, matrix, S if matrix is None else widths_[0], start, stop)

            def attention(scores, values):
                g0 = k["heads"]
                def score(g):
                    if g >= 2:
                        pe.wait_ge(biased, 2 * (g - 2) + 1)
                    for j in range(2):
                        q, key = scores(g - g0, j)
                        last = nc.tensor.matmul(bank[g % 2][:, j * S:(j + 1) * S], q, key, start=True, stop=True)
                    last.then_inc(score_done, 1)

                def transpose(g):
                    pe.wait_ge(scaled, 3 * g + 3)
                    if g >= 2:
                        pe.wait_ge(ptc_done, g - 1)
                    for kt in range(2):
                        for j in range(2):
                            last = nc.tensor.transpose(bank[2 + g % 2][:, kt * S + j * P:kt * S + (j + 1) * P],
                                                       sc_buf[:, g % 3, j * S + kt * P:j * S + (kt + 1) * P], ident)
                    last.then_inc(pt_done, 1)

                def value(g):
                    p_, side = g // 2, g % 2
                    pe.wait_ge(ptc_done, g + 1)
                    if side == 0 and p_ >= 2:
                        pe.wait_ge(yev_done, p_ - 1)
                    for kt in range(2):
                        last = nc.tensor.matmul(bank[4 + p_ % 2][64 * side:64 * side + 64, 0:S], values(g - g0, kt),
                                                pt_buf[:, g % 2, kt * S:(kt + 1) * S], start=kt == 0, stop=kt == 1)
                    last.then_inc(pv_done, 1)

                score(g0)
                score(g0 + 1)
                for g in range(g0, g0 + 16):
                    if g + 2 < g0 + 16:
                        score(g + 2)
                    transpose(g)
                    if g > g0:
                        value(g - 1)
                value(g0 + 15)
                k["heads"] += 16

            def ffn(c0):
                T0 = k["ffn"] * FT

                def up(t, c, slot_c):
                    pe.wait_ge(lo_done, c + 1)
                    if not isinstance(t, int) or t >= 3:
                        pe.wait_ge(up_ready, t + (T0 - 1))
                    for m in range(2):
                        for kt in range(8):
                            if isinstance(t, int) and t == 0 and m == 0:
                                pe.wait_ge(hlo_done, k["hlo"] + kt + 1)
                            last = product(bank[slot_c % 3][:, m * S:(m + 1) * S], weights(slot_c, (8 * m + kt) * P),
                                           h_parts(kt), kt == 0, kt == 7)
                        if isinstance(t, int) and t == 0 and m == 0:
                            sum_squares([512] * 2, stop=False)
                    last.then_inc(chunk_used, 1)

                def down(i, c, slot_c, first=False, last_=False):
                    pe.wait_ge(lo_done, c + 1)
                    pe.wait_ge(ulo_done, i * 2 + (T0 + 2))
                    for m in range(8):
                        for a in range(2):
                            last = product(bank[DOWN0 + m // 2][:, (m % 2) * S:(m % 2 + 1) * S],
                                           weights(slot_c, a * D + m * P), h_parts(8 + a),
                                           first and a == 0 and m % 2 == 0, last_ and a == 1, skip_group_check=True)
                        if last_ and m in (1, 3, 5):
                            last.then_inc(sum_ready, 1)
                    last.then_inc(chunk_used, 1)

                up(0, c0, c0)
                sum_squares([512] * 2, start=False)
                up(1, c0 + 1, c0 + 1)
                up(2, c0 + 2, c0 + 2)
                up(3, c0 + 3, c0 + 3)
                down(0, c0 + 4, c0 + 4, first=True)
                with pe.Fori(2, FT // 2) as i:
                    for a in range(2):
                        up(i * 2 + a, i * 3 + (c0 - 1 + a), c0 + 2 + a)
                    down(i - 1, i * 3 + (c0 + 1), c0 + 4)
                down(FT // 2 - 1, c0 + 32, c0 + 32, last_=True)
                k["hlo"] += 8
                k["ffn"] += 1

            pe.wait_ge(consts_loaded, 32)
            for name in stages:
                c0 = first_chunk[name]
                if not name.startswith("ffn"):
                    sum_squares([512] * 4)
                e0 = k["evac"]
                if name == "mix":
                    for c in range(9):
                        free = (evac_done, e0 + c - 2) if c >= 3 else None
                        if 4 <= c < 6:
                            token_chunk(c0 + c, free=free)
                        else:
                            feature_chunk(c0 + c, wait_h=k["hlo"] if c == 0 else None, free=free)
                    k["hlo"] += 8
                    sum_squares([S] * 3)
                    sum_squares([S] * 2)
                    for c in range(9, 19):
                        free = (evac_done, e0 + c - 2)
                        if 12 <= c < 16:
                            pe.wait_ge(rope_step, 3 * (c - 12) + 2)
                        if c < 13:
                            feature_chunk(c0 + c, 8, 3, 2, k["hlo"] if c == 9 else None, free)
                        elif c < 17:
                            feature_chunk(c0 + c, 11, 2, 2, k["hlo"] + 3 if c == 13 else None, free)
                        else:
                            token_chunk(c0 + c, 11, 2, free)
                    k["hlo"] += 5
                    k["evac"] += 19
                    pe.wait_ge(evac_done, k["evac"])
                    pe.wait_ge(rope_step, 15)

                    def mix_scores(h, j):
                        if h < HA:
                            r = slice(64 * (h % 2), 64 * (h % 2) + 64)
                            return qk_a[r, h // 2, j * P:(j + 1) * P], qk_a[r, 4 + h // 2, :]
                        h -= HA
                        return q_b[0:96, h, j * P:(j + 1) * P], k_b[0:96, h, :]

                    attention(mix_scores, lambda h, kt: (v_a if h < HA else v_b)[:, kt, 64 * (h % 8):64 * (h % 8) + 64])
                    sum_squares([S] * 4)
                    sum_squares([S] * 4)
                    for c in range(19, 23):
                        feature_chunk(c0 + c, wait_h=k["hlo"] if c == 19 else None,
                                      free=(evac_done, k["evac"] + 1) if c == 22 else None)
                    k["hlo"] += 8
                    k["evac"] += 4
                    sum_squares([512] * 4)
                elif name.startswith("ffn"):
                    ffn(c0)
                    if name == "ffn0":
                        sum_squares([512] * 4)
                        k["evac"] += 4
                elif name.startswith("conv"):
                    def tap_products(p_):
                        pe.wait_ge(glu_done, k["glu"] + 2 * p_ + 2)
                        for m in (2 * p_, 2 * p_ + 1):
                            pe.wait_ge(diag_done, k["diag"] + m + 1)
                            for tap in pe_taps(m):
                                last = nc.tensor.matmul(half_bank(m), diag[:, diag_slot(m, tap), :], u_pad[:, m, tap:tap + S],
                                                        start=tap == CW - PE_TAPS[m], stop=tap == CW - 1)
                        last.then_inc(pe_taps_done, 1)

                    if k["x"]:
                        pe.wait_ge(x_ready, k["x"])
                    for c in range(8):
                        feature_chunk(c0 + c, wait_h=k["hlo"] if c == 0 else None,
                                      free=(glu_done, k["glu"] + c - 2) if c >= 3 else None)
                        if c >= 2 and c % 2 == 0:
                            tap_products(c // 2 - 1)
                    tap_products(3)
                    k["glu"] += 8
                    k["hlo"] += 8
                    k["diag"] += 8
                    n_steps = [sum(CW - PE_TAPS[n] + 1 for n in range(m // 2 * 2 + 2)) for m in range(8)]
                    sums([([c_acc[:, m, :]], conv_step, k["conv"] + n_steps[m]) for m in range(8)])
                    k["conv"] += n_steps[7]
                    sum_squares([512] * 4)
                    for c in range(8, 12):
                        feature_chunk(c0 + c, wait_h=k["hlo"] if c == 8 else None,
                                      free=(x_ready, k["x"] + 1) if c == 11 else None)
                    k["hlo"] += 8
                elif name == "nat":
                    def flip(n):
                        pe.wait_ge(table_masked, n + 1)
                        if n >= 4:
                            pe.wait_ge(table_step, n - 3)
                        nc.tensor.matmul(bank[DOWN0 + n % 4][:, :], cc("flip", P), t_up[:, n * 512:(n + 1) * 512],
                                         start=True, stop=True).then_inc(flipped, 1)

                    for n in range(4):
                        flip(n)
                    for c in range(12):
                        free = (evac_done, e0 + c - 2) if c >= 3 else None
                        if c < 8:
                            feature_chunk(c0 + c, wait_h=k["hlo"] if c == 0 else None, free=free)
                        else:
                            token_chunk(c0 + c, free=free)
                        if 1 <= c <= 8:
                            sum_squares([512], half_ones)
                        if c < 8:
                            flip(4 + c)
                    k["hlo"] += 8
                    k["evac"] += 12
                    pe.wait_ge(evac_done, k["evac"])
                    pe.wait_ge(nq_done, 8)

                    def nat_scores(h, j):
                        r = slice(64 * (h % 2), 64 * (h % 2) + 64)
                        return qk_n[r, h // 2, j * P:(j + 1) * P], qk_n[r, 8 + h // 2, :]

                    attention(nat_scores, lambda h, kt: v_n[:, kt, 64 * h:64 * h + 64])
                    for c in range(12, 16):
                        feature_chunk(c0 + c, wait_h=k["hlo"] if c == 12 else None,
                                      free=(x_ready, k["x"] + 1) if c == 15 else None)
                    k["hlo"] += 8
                elif name == "ret":
                    for c in range(24):
                        if c < 3:
                            free = None
                        elif c < 11:
                            free = (rot_v, 2 * (c - 3) + 2)
                        else:
                            free = (evac_done, e0 + c - 10)
                        if 8 <= c < 16:
                            token_chunk(c0 + c, free=free)
                        else:
                            feature_chunk(c0 + c, wait_h=k["hlo"] if c == 0 else None, free=free)
                    k["hlo"] += 8
                    k["evac"] += 16
                    pe.wait_ge(evac_done, k["evac"])
                    pe.wait_ge(rot_p, 16)

                    def score(h):
                        if h >= 2:
                            pe.wait_ge(prob_done, h - 1)
                        for jt in range(2):
                            for d in range(2):
                                last = nc.tensor.matmul(bank[h % 2][:, jt * S:(jt + 1) * S],
                                                        k_r[:, 2 * h + d, jt * P:(jt + 1) * P], q_r[:, 2 * h + d, :],
                                                        start=d == 0, stop=d == 1)
                        last.then_inc(score_done, 1)

                    def output(h):
                        pe.wait_ge(prob_done, h + 1)
                        if h >= 2:
                            pe.wait_ge(evac_done, k["evac"] + 2 * (h - 2) + 2)
                        for e in range(4):
                            for jt in range(2):
                                last = nc.tensor.matmul(bank[3 + 2 * (h % 2) + e // 2][:, (e % 2) * S:(e % 2 + 1) * S],
                                                        v_r[:, jt, h * RVD + e * P:h * RVD + (e + 1) * P],
                                                        p_r[:, h % 2, jt * S:(jt + 1) * S], start=jt == 0, stop=jt == 1)
                            if e % 2:
                                last.then_inc(ret_out, 1)

                    score(0)
                    for h in range(RH):
                        if h + 1 < RH:
                            score(h + 1)
                        output(h)
                    k["heads"] += 4
                    for h in range(RH):
                        sums([([o_ret(h, 2 * e), o_ret(h, 2 * e + 1)], evac_done, k["evac"] + 2 * h + e + 1) for e in range(2)])
                        sum_squares([512] * 2)
                    k["evac"] += 8
                    for c in range(24, 32):
                        feature_chunk(c0 + c, 0, 16, 1, k["hlo"] if c == 24 else None,
                                      (x_ready, k["x"] + (c - 26) // 2) if c >= 28 else None)
                    k["hlo"] += 16
                k["x"] += 4


def split_columns(w, cols):
    return w[:, cols].reshape(w.shape[0] // P, P, len(cols)).transpose(1, 0, 2)


def pack_weights(a, stages=ALL_STAGES):
    n = sum(len(chunk_widths(s)) for s in stages) + 1
    out = np.zeros((n, P, CH), np.float32)
    at = 0

    def put(*blocks):
        nonlocal at
        flat = np.concatenate([b.reshape(P, -1) for b in blocks], 1)
        out[at, :, :flat.shape[1]] = flat
        at += 1

    def tiles(w, *cols):
        put(*[split_columns(w, c) for c in cols])

    def span(a0, n=P):
        return np.arange(a0, a0 + n)

    def columns(w, n_chunks):
        for c in range(n_chunks):
            tiles(w, span(2 * c * P), span((2 * c + 1) * P))

    for s in stages:
        if s == "mix":
            w = a["w_in"][0]
            columns(w, 4)
            for c in range(2):
                tiles(w, span(2 * 512 + c * 256, 256))
            q0, kv0, r0 = 3 * 512, 3 * 512 + QL, 3 * 512 + QL + KL
            swap = np.concatenate([np.arange(16, 32), np.arange(16)])
            key = np.concatenate([np.arange(32), np.arange(32), np.arange(32), swap]) + r0
            tiles(w, span(q0), span(q0 + P))
            tiles(w, span(q0 + 2 * P), span(kv0))
            tiles(w, span(kv0 + P), key)
            head = np.concatenate([np.arange(NOPE + ROPE), NOPE + swap])
            for c in range(4):
                tiles(a["w_uq"][0], *[(NOPE + ROPE) * h + head for h in (2 * c, 2 * c + 1)])
            for c in range(4):
                tiles(a["w_ukv"][0], *[span(P * h) for h in (2 * c, 2 * c + 1)])
            values = np.concatenate([span(P * h + 64, 64) for h in range(HB)])
            for c in range(2):
                tiles(a["w_ukv"][0], values[256 * c:256 * c + 256])
            columns(a["w_o"][0], 4)
        elif s.startswith("ffn"):
            i = int(s[3:])
            up = a["w_up"][0] if i == 0 else a["ffn_w_up_2"][i - 1]
            down = a["w_down"][0] if i == 0 else a["ffn_w_down_2"][i - 1]
            ups = up.reshape(8, P, 2, FT, P)[:, :, ::-1 if i else 1]
            ups = ups.transpose(3, 1, 2, 0, 4).reshape(FT, P, CH)
            downs = down.reshape(FT // 2, 2, P, D).transpose(0, 2, 1, 3).reshape(FT // 2, P, CH)
            order = [ups[0], ups[1]]
            for b in range(1, FT // 2):
                order += [ups[2 * b], ups[2 * b + 1], downs[b - 1]]
            order.append(downs[FT // 2 - 1])
            for block_ in order:
                out[at] = block_
                at += 1
        elif s.startswith("conv"):
            j = int(s[4:])
            w = a["conv_w_in_2"][j]
            for m in range(8):
                tiles(w, span(m * P), span(D + m * P))
            columns(a["conv_w_out_2"][j], 4)
        elif s == "nat":
            w = a["nat_w_qkv_2"][0]
            columns(w, 8)
            for c in range(4):
                tiles(w, span(2 * D + 256 * c, 256))
            columns(a["nat_w_out_2"][0], 4)
        else:
            w = a["ret_w_in_2"][0]
            for h in range(RH):
                for part in range(2):
                    tiles(w, span(part * D + 2 * h * P), span(part * D + (2 * h + 1) * P))
            for c in range(8):
                tiles(w, span(2 * D + 256 * c, 256))
            for c in range(8):
                tiles(w, span(2 * D + 2048 + 2 * c * P), span(2 * D + 2048 + (2 * c + 1) * P))
            for m in range(8):
                tiles(a["ret_w_out_2"][0], span(m * P))
    assert at == n - 1
    return out


def pack_params(a):
    at, n = param_layout()
    out = np.zeros((P, n), np.float32)

    def put(name, v):
        v = v.reshape(-1, P).T
        out[:, at[name]:at[name] + v.shape[1]] = v

    for name in ("norm_mix_pre", "q_lat_norm", "kv_lat_norm", "out_norm_a", "out_norm_b", "norm_mix_post", "norm_ffn_pre",
                 "norm_ffn_post", "norm1_g_2", "norm2_g_2", "conv_b_in_2", "conv_dw_b_2", "conv_ln_g_2", "conv_ln_b_2",
                 "ret_gn_g_2"):
        put(name, a[name])
    put("conv_dw_w_2", a["conv_dw_w_2"].reshape(2, CW, 8, P).transpose(0, 2, 1, 3))
    for name in ("nat_q_norm_g_2", "nat_k_norm_g_2"):
        put(name, np.tile(a[name], (1, 2)))
    o = at["ret_log2_inv_decay_2"]
    out[:, o:o + 8] = a["ret_log2_inv_decay_2"].reshape(1, 8)
    taps = np.concatenate([a["conv_w"], a["ffn_dw_w_2"]]).reshape(5, 3, 2, FT, P)
    bias = np.concatenate([a["conv_b"], a["ffn_dw_b_2"]]).reshape(5, 1, 2, FT, P)
    both = np.concatenate([taps, bias], 1).transpose(0, 3, 2, 1, 4)
    put("ffn_dw", np.concatenate([both[:1], both[1:, :, ::-1]]))
    return out


def lay_out(inputs, stages=ALL_STAGES):
    a = {name: np.asarray(v) for name, v in inputs.items()}
    rpb = np.zeros((NH, 15, P), np.float32)
    rpb[:, :, GW - KW:GW + KW - 1] = a["nat_rpb_2"][0]
    return {
        "wstream": pack_weights(a, stages),
        "x_in": np.ascontiguousarray(a["x"][0].T.reshape(DT, P, S)),
        "params": pack_params(a),
        "consts": build_constants(),
        "dilated_bias": dilated_bias(),
        "rpb": rpb,
    }


def declare(nc, arrays, stages=ALL_STAGES):
    args = [nc.dram_tensor(name, v.shape, F32, kind="ExternalInput").ap() for name, v in arrays.items()]
    args.append(nc.dram_tensor("x_out", (DT, P, S), F32, kind="ExternalOutput").ap())
    build_program(nc, *args, stages=stages)


def kernel(**inputs):
    import concourse.bacc as bacc
    from concourse.bass_utils import run_bass_kernel_spmd

    arrays = lay_out(inputs)
    nc = bacc.Bacc("TRN2", target_bir_lowering=False, num_devices=1)
    declare(nc, arrays)
    r = run_bass_kernel_spmd(nc, [arrays], core_ids=[0])
    return np.ascontiguousarray(r.results[0]["x_out"].reshape(1, D, S).transpose(0, 2, 1))
```

```python
import math

import numpy as np

import concourse.bass as bass
from concourse import mybir
from collections import Counter
from contextlib import ExitStack

F32 = mybir.dt.float32
F32R = mybir.dt.float32r
ACT = mybir.ActivationFunctionType
ALU = mybir.AluOpType
AX = mybir.AxisListType

P = 128
S = 256
D = 1024
DT = D // P
CH = 2048
RING = 3
FF = 2816
FT = FF // P
EPS = 1e-6
NEG = -1e30
HA, HDA = 8, 64
HB, NOPE, ROPE = 8, 64, 32
QL, KL = 384, 256
NH, NHD = 16, 64
GW, KW = 64, 16
RH, RKD, RVD = 4, 256, 512
CW = 31
PADC = CW // 2
RET_SUMS = [("mean", 0), ("mean", 1), ("var", 0), ("mean", 2), ("mean", 3), ("var", 1), ("var", 2), ("var", 3)]
PE_TAPS = (11, 11, 11, 11, 11, 11, 14, 14)

ALL_STAGES = ("mix", "ffn0", "conv0", "ffn1", "nat", "ffn2", "ret", "ffn3", "conv1", "ffn4")


def chunk_widths(name):
    if name == "mix":
        return [CH] * 9 + [2 * 3 * P] * 4 + [2 * 2 * P] * 4 + [2 * 256] * 2 + [CH] * 4
    if name.startswith("ffn"):
        return [CH] * (FT + FT // 2)
    if name.startswith("conv"):
        return [CH] * (8 + 4)
    if name == "nat":
        return [CH] * (8 + 4 + 4)
    return [CH] * (8 + 8 + 8 + 8)


def param_layout():
    at, off = {}, 0
    for name, n in (("norm_mix_pre", 8), ("q_lat_norm", 3), ("kv_lat_norm", 2), ("out_norm_a", 4),
                    ("out_norm_b", 4), ("norm_mix_post", 8), ("norm_ffn_pre", 8), ("norm_ffn_post", 8),
                    ("norm1_g_2", 32), ("norm2_g_2", 32), ("conv_b_in_2", 32), ("conv_dw_w_2", 2 * 8 * CW),
                    ("conv_dw_b_2", 16), ("conv_ln_g_2", 16), ("conv_ln_b_2", 16), ("nat_q_norm_g_2", 1),
                    ("nat_k_norm_g_2", 1), ("ret_log2_inv_decay_2", 8), ("ret_gn_g_2", 16),
                    ("ffn_dw", 5 * FT * 2 * 4)):
        at[name] = off
        off += n
    return at, off


def const_layout():
    at, off = {}, 0
    for name, n in (("ident", P), ("ones", P), ("half_ones", P), ("rope_cos", S), ("rope_sin", S),
                    ("rot_cos", S), ("rot_sin", S), ("fwd", 2 * S), ("bwd", 2 * S), ("nat_mask", GW), ("flip", P)):
        at[name] = off
        off += n
    return at, off


def build_constants():
    at, n = const_layout()
    c = np.zeros((P, n), np.float32)
    c[:, at["ident"]:at["ident"] + P] = np.eye(P)
    c[:, at["ones"]:at["ones"] + P] = 1.0
    for g in range(2):
        c[64 * g:64 * g + 64, at["half_ones"] + 64 * g:at["half_ones"] + 64 * g + 64] = 1.0
        flip = slice(at["flip"] + 64 * g, at["flip"] + 64 * g + 64)
        c[64 * g:64 * g + 64, flip] = np.eye(64)[::-1]
    pos = np.arange(S, dtype=np.float32)
    inv = np.exp(np.float32(-math.log(10000.0)) * np.arange(0, ROPE, 2, dtype=np.float32) / np.float32(ROPE)).astype(np.float32)
    ang = (pos[:, None] * inv[None, :]).astype(np.float32).T
    cos, sin = np.cos(ang).astype(np.float32), np.sin(ang).astype(np.float32)
    c[64:96, at["rope_cos"]:at["rope_cos"] + S] = np.concatenate([cos, cos])
    c[96:128, at["rope_sin"]:at["rope_sin"] + S] = np.concatenate([-sin, sin])
    theta = (1.0 / (np.float32(10000.0) ** np.linspace(0.0, 1.0, 128, dtype=np.float32))).astype(np.float32)
    ang = (pos[:, None] * theta[None, :]).astype(np.float32).T
    c[:, at["rot_cos"]:at["rot_cos"] + S] = np.cos(ang)
    c[:, at["rot_sin"]:at["rot_sin"] + S] = np.sin(ang)
    j = np.arange(S)[:, None]
    i = np.arange(S)[None, :]
    for name, m in (("fwd", np.maximum(i - j, 0)), ("bwd", np.maximum(j - i, 0))):
        c[:, at[name]:at[name] + 2 * S] = m.reshape(2, P, S).transpose(1, 0, 2).reshape(P, 2 * S)
    col = np.arange(GW)
    start = np.clip(col - KW // 2, 0, GW - KW)
    inside = (col[None, :] >= start[:, None]) & (col[None, :] < start[:, None] + KW)
    c[:, at["nat_mask"]:at["nat_mask"] + GW] = np.tile(np.where(inside, 0.0, NEG)[::-1], (2, 1))
    return c


def dilated_bias():
    t, s = np.arange(S)[:, None], np.arange(S)[None, :]
    dist = np.abs(t - s)
    count = np.zeros((S, S))
    for window, r in ((128, 1), (512, 4), (2048, 16)):
        count += (dist % r == 0) & (dist // r <= window // (2 * r))
    log_count = np.where(count > 0, np.log(np.maximum(count, 1)), NEG)
    out = np.empty((P, HA, 2, S), np.float32)
    for h in range(HA):
        slope = 2.0 ** (-8.0 * (h + 1) / HA)
        out[:, h] = (-slope * dist + log_count).reshape(2, P, S).transpose(1, 0, 2)
    return out.reshape(P, -1)


def build_program(nc, wstream, x_in, params_in, consts_in, bias_in, rpb_in, out, stages=ALL_STAGES):
    PA, NP_ = param_layout()
    CA, NC_ = const_layout()
    FIRST = CA["rope_cos"]
    widths, first_chunk = [], {}
    for name in stages:
        first_chunk[name] = len(widths)
        widths += chunk_widths(name)
    widths.append(CH)
    n_chunks = len(widths)
    second_chunks = [c + 1 for c in first_chunk.values()]

    with ExitStack() as ctx:
        def sb(name, shape, dt=F32):
            return ctx.enter_context(nc.sbuf_tensor(name, shape, dt))

        def sem(name):
            return ctx.enter_context(nc.semaphore(name))

        raw = sb("raw", [P, RING, CH])
        w_hi = sb("w_hi", [P, RING, CH], F32R)
        w_lo = sb("w_lo", [P, RING, CH], F32R)
        x = sb("x", [P, DT, S])
        h_hi = sb("h_hi", [P, 16, S], F32R)
        h_lo = sb("h_lo", [P, 16, S], F32R)
        par = sb("par", [P, NP_])
        cst = sb("cst", [P, NC_])
        hn = sb("hn", [P, 2, S])
        sq = sb("sq", [P, 2, 2 * S])
        rs_v = sb("rs_v", [P, 2 * S])
        rs_y = sb("rs_y", [P, 2 * S])
        rs_t = sb("rs_t", [P, 2 * S])
        neg_max = sb("neg_max", [P, 4])
        z_sum = sb("z_sum", [P, 4])
        z_inv = sb("z_inv", [P, 4])
        ARENA = 16896
        arena = sb("arena", [P, ARENA])
        bank = [ctx.enter_context(nc.psum_tensor(f"bank{i}", [P, 512], F32)) for i in range(8)]
        stat = bank[7]
        DOWN0 = 3

        raw_full = [sem(f"raw_full{i}") for i in range(RING)]
        bias_full = [sem(f"bias_full{i}") for i in range(2)]
        tables_loaded = sem("tables_loaded")
        x_loaded, consts_loaded, rpb_loaded, stored = sem("x_loaded"), sem("consts_loaded"), sem("rpb_loaded"), sem("stored")
        hi_done, lo_done, chunk_used = sem("hi_done"), sem("lo_done"), sem("chunk_used")
        x_ready = sem("x_ready")
        sq_done, sum_done, stat_read = sem("sq_done"), sem("sum_done"), sem("stat_read")
        ars_done, newton = sem("ars_done"), sem("newton")
        hn_done, hhi_done, hlo_done = sem("hn_done"), sem("hhi_done"), sem("hlo_done")
        evac_done = sem("evac_done")
        up_ready = sem("up_ready")
        sum_ready = sem("sum_ready")
        lin_done, taps_done, gelu_done = sem("lin_done"), sem("taps_done"), sem("gelu_done")
        prod_done, uhi_done, ulo_done = sem("prod_done"), sem("uhi_done"), sem("ulo_done")
        score_done, biased, exp_done, scaled = sem("score_done"), sem("biased"), sem("exp_done"), sem("scaled")
        pt_done, ptc_done, pv_done, yev_done = sem("pt_done"), sem("ptc_done"), sem("pv_done"), sem("yev_done")
        rope_step, post_step, nq_done = sem("rope_step"), sem("post_step"), sem("nq_done")
        table_masked, table_step = sem("table_masked"), sem("table_step")
        diag_done, pe_taps_done = sem("diag_done"), sem("pe_taps_done")
        gate_done, glu_done, pad_done, conv_step = sem("gate_done"), sem("glu_done"), sem("pad_done"), sem("conv_step")
        mean_read = sem("mean_read")
        centred, silu_done = sem("centred"), sem("silu_done")
        rot_v, rot_p = sem("rot_v"), sem("rot_p")
        dec_v, dec_a, mask_v, mask_a, prob_done = sem("dec_v"), sem("dec_a"), sem("mask_v"), sem("mask_a"), sem("prob_done")
        ret_out, gated, flipped = sem("ret_out"), sem("gated"), sem("flipped")

        def pe_taps(m):
            return range(CW - PE_TAPS[m], CW)

        def half_bank(m):
            return bank[DOWN0 + m // 2][:, (m % 2) * S:(m % 2 + 1) * S]

        def diag_slot(m, tap):
            return sum(PE_TAPS[:m]) + tap - (CW - PE_TAPS[m])

        def cc(name, n, p0=0, p1=P):
            return cst[p0:p1, CA[name]:CA[name] + n]

        def pcol(name, i=0):
            return par[:, PA[name] + i:PA[name] + i + 1]

        def pair(view, t):
            return view[:, 2 * t:2 * t + 2, :].rearrange("p a b -> p (a b)")

        def halves(view):
            return view.rearrange("p (a b) -> p a b", a=2)

        def region(off, *dims):
            n = int(np.prod(dims))
            assert off + n <= ARENA, (off, n)
            v = arena[:, off:off + n]
            if len(dims) == 2:
                v = v.rearrange("p (a b) -> p a b", a=dims[0])
            return v

        sc_buf = region(0, 3, 512)
        pt_buf = region(1536, 2, 512)
        y_att = region(2560, 8, S)
        A0 = 4608
        qk_a = region(A0, 8, S)
        v_a = region(A0 + 2048, 2, 512)
        lat = region(A0 + 3072, 6, S)
        q_b = region(A0 + 4608, HB, S)
        k_b = region(A0 + 6656, HB, S)
        v_b = region(A0 + 8704, 2, 512)
        rope_t = region(A0 + 9728, 2, 512)
        bias_a = region(A0 + 10752, 2, 512)
        qk_n = region(A0, 16, S)
        v_n = region(A0 + 4096, 2, D)
        t_n = region(A0 + 6144, NH * 6 * GW)
        t_up = region(A0, NH * 6 * GW)
        lin = region(0, 2, 512)
        u32 = region(1024, 2, S)
        up_n = region(1536, 2, 512)
        y_post = region(2560, 8, S)
        UP = S + 2 * PADC
        u_pad = region(0, DT, UP)
        c_acc = region(DT * UP, DT, S)
        c_sg = region(DT * (UP + S), 2, S)
        DG0 = DT * (UP + S) + 2 * S
        diag = region(DG0, (ARENA - DG0) // P, P)
        q_r, k_r = region(0, 8, S), region(2048, 8, S)
        v_r, g_r = region(4096, 2, 2048), region(8192, 16, S)
        p_r, d_r, rot = region(12288, 2, 512), region(13312, 2, 512), region(14336, 4, 512)
        dec = region(16384, 8, 8)

        def o_ret(h, e):
            return (q_r if e < 2 else k_r)[:, 2 * h + e % 2, :]

        block = ctx.enter_context(nc.Block())

        @block.sync
        def _(sp):
            def load(c):
                if c >= RING:
                    sp.wait_ge(lo_done, c - RING + 1)
                sp.dma_start(raw[:, c % RING, 0:widths[c]], wstream[c, :, 0:widths[c]]).then_inc(raw_full[c % RING], 16)

            sp.dma_start(x[:, :, :], x_in.rearrange("t p s -> p t s")).then_inc(x_loaded, 16)
            sp.dma_start(cst[:, 0:FIRST], consts_in[:, 0:FIRST]).then_inc(consts_loaded, 16)
            sp.dma_start(par[:, :], params_in).then_inc(consts_loaded, 16)
            load(0)
            load(1)
            sp.dma_start(cst[:, FIRST:NC_], consts_in[:, FIRST:NC_]).then_inc(tables_loaded, 16)
            uneven = max([c + 1 for c in range(n_chunks) if widths[c] != CH] + [RING])
            start = -(-uneven // RING)
            end = n_chunks // RING
            for c in range(2, start * RING):
                load(c)
            with sp.Fori(start, end) as i:
                for s in range(RING):
                    sp.wait_ge(lo_done, i * RING + (s - RING + 1))
                    sp.dma_start(raw[:, s, :], wstream[bass.ds(i * RING + s, 1)].rearrange("a p n -> (a p) n"))\
                      .then_inc(raw_full[s], 16)
            for c in range(end * RING, n_chunks):
                load(c)
            sp.wait_ge(x_ready, 4 * len(stages))
            sp.dma_start(out.rearrange("t p s -> p t s"), x[:, :, :]).then_inc(stored, 16)
            for s in range(RING):
                sp.wait_ge(raw_full[s], 16 * len(range(s, n_chunks, RING)))
            sp.wait_ge(stored, 16)

        @block.gpsimd
        def _(pool):
            k = Counter()

            def diagonals(j):
                for m in range(DT):
                    for tap in pe_taps(m):
                        ins = nc.gpsimd.tensor_scalar(diag[:, diag_slot(m, tap), :], cc("ident", P),
                                                      pcol("conv_dw_w_2", (8 * j + m) * CW + tap), None, ALU.mult)
                    ins.then_inc(diag_done, 1)

            def bias_table():
                for h in range(NH):
                    for half in range(2):
                        src = bass.AP(tensor=rpb_in.tensor, offset=rpb_in[h, 5 - half:6 - half, 0:1].offset,
                                      ap=[[1, GW], [P, 6], [1, GW]])
                        dst = t_up[64 * half:64 * half + 64, h * 6 * GW:(h + 1) * 6 * GW]
                        pool.dma_start(dst.rearrange("p (a b) -> p a b", a=6), src).then_inc(rpb_loaded, 16)
                pool.wait_ge(rpb_loaded, 16 * 2 * NH)
                mask = cc("nat_mask", GW).unsqueeze(1).broadcast_to([P, 8, GW])
                for n in range(12):
                    part = t_up[:, n * 512:(n + 1) * 512].rearrange("p (a b) -> p a b", b=GW)
                    nc.gpsimd.tensor_tensor(part, part, mask, ALU.add).then_inc(table_masked, 1)

            pool.wait_ge(consts_loaded, 32)
            pool.wait_ge(tables_loaded, 16)
            for name in stages:
                c0 = first_chunk[name]
                if name == "mix":
                    for h in range(HA):
                        if h >= 2:
                            pool.wait_ge(biased, 2 * (h - 2) + 1)
                        pool.dma_start(bias_a[:, h % 2, :], bias_in[:, h * 512:(h + 1) * 512]).then_inc(bias_full[h % 2], 16)
                if name.startswith("conv"):
                    if c0 == 0:
                        diagonals(int(name[4:]))
                    if k["x"]:
                        pool.wait_ge(x_ready, k["x"])
                    nc.gpsimd.memset(u_pad[:, :, 0:PADC], 0.0).then_inc(pad_done, 1)
                    nc.gpsimd.memset(u_pad[:, :, PADC + S:UP], 0.0).then_inc(pad_done, 1)
                if name == "nat" and c0 == 0:
                    bias_table()
                if name == "ret":
                    for c in range(8):
                        dst = (k_r if c % 2 else q_r)[:, 2 * (c // 2):2 * (c // 2) + 2, :]
                        a, b = rot[:, 2 * (c % 2), :], rot[:, 2 * (c % 2) + 1, :]
                        pool.wait_ge(rot_v, k["rot_v"] + 2 * c + 2)
                        nc.gpsimd.tensor_tensor(dst[:, 0, :], a[:, 0:S], b[:, S:2 * S], ALU.subtract).then_inc(rot_p, 1)
                        nc.gpsimd.tensor_tensor(dst[:, 1, :], b[:, 0:S], a[:, S:2 * S], ALU.add).then_inc(rot_p, 1)
                    k["rot_v"] += 16
                after = stages[stages.index(name) + 1:][:1]
                if after and after[0].startswith("conv"):
                    if k["x"]:
                        pool.wait_ge(x_ready, k["x"])
                    diagonals(int(after[0][4:]))
                if after == ("nat",):
                    if k["x"]:
                        pool.wait_ge(x_ready, k["x"])
                    bias_table()
                k["x"] += 4

        @block.scalar
        def _(act):
            k = Counter()

            def split_hi(c, second=False):
                if c >= n_chunks or c in second_chunks and not second:
                    return
                w = widths[c]
                act.wait_ge(raw_full[c % RING], 16 * (c // RING + 1))
                if c >= RING:
                    act.wait_ge(chunk_used, c - RING + 1)
                nc.scalar.activation(w_hi[:, c % RING, 0:w], raw[:, c % RING, 0:w], ACT.Copy).then_inc(hi_done, 1)

            def squares(sources, summed=None):
                for e, (view, width, ready, value) in enumerate(sources):
                    g = k["sq"]
                    act.wait_ge(ready, value)
                    if g >= 2:
                        act.wait_ge(sum_done, k["sum"] - 1 if summed is None else summed + e)
                    nc.scalar.activation(sq[:, g % 2, 0:width], view, ACT.Square).then_inc(sq_done, 1)
                    k["sq"] += 1
                    k["sum"] += 1

            def inv_sqrt(width=S):
                k["stat"] += 1
                act.wait_ge(stat_read, k["stat"])
                nc.scalar.activation(rs_y[:, 0:width], rs_v[:, 0:width], ACT.Abs_reciprocal_sqrt).then_inc(ars_done, 1)

            def split_h(tiles, silu=None):
                for i, t in enumerate(tiles):
                    act.wait_ge(hn_done, k["hn"] + 1)
                    h = hn[:, k["slot"] % 2, :]
                    if silu:
                        nc.scalar.activation(h, h, ACT.Silu, bias=silu(i)).then_inc(silu_done, 1)
                        k["silu"] += 1
                        act.wait_ge(silu_done, k["silu"])
                    nc.scalar.activation(h_hi[:, t, :], h, ACT.Copy).then_inc(hhi_done, 1)
                    k["hn"] += 1
                    k["slot"] += 1

            def evac(c, dst, src, func=ACT.Copy):
                act.wait_ge(chunk_used, c + 1)
                nc.scalar.activation(dst, src, func).then_inc(evac_done, 1)
                k["evac"] += 1

            def x_pairs(a, b):
                return [(pair(x, t), 512) + ((x_ready, k["x"] - 3 + t) if k["x"] else (x_loaded, 16)) for t in range(a, b)]

            def prenorm(c0):
                if c0:
                    split_hi(c0 + 1, second=True)
                squares(x_pairs(0, 4))
                inv_sqrt()
                if c0 == 0:
                    split_hi(0)
                    split_hi(1, second=True)
                split_h(range(DT))

            def y_evac(p_):
                act.wait_ge(pv_done, 2 * p_ + 2)
                nc.scalar.activation(y_att[:, p_ % 8, :], bank[4 + p_ % 2][:, 0:S], ACT.Copy).then_inc(yev_done, 1)

            def attention(between=None):
                g0 = k["heads"]
                for g in range(g0, g0 + 17):
                    if g < g0 + 16:
                        act.wait_ge(biased, 2 * g + 2)
                        if g >= 2:
                            act.wait_ge(scaled, 3 * (g - 2) + 1)
                        for j in range(2):
                            i = 2 * (g % 2) + j
                            view = sc_buf[:, g % 3, j * S:(j + 1) * S]
                            nc.scalar.activation(view, view, ACT.Exp, bias=neg_max[:, i:i + 1],
                                                 accum_out=z_sum[:, i:i + 1]).then_inc(exp_done, 1)
                    if g > g0:
                        act.wait_ge(pt_done, g)
                        if g - 1 >= 2:
                            act.wait_ge(pv_done, g - 2)
                        nc.scalar.activation(pt_buf[:, (g - 1) % 2, :], bank[2 + (g - 1) % 2][:, :], ACT.Copy)\
                                 .then_inc(ptc_done, 1)
                    if g >= g0 + 3 and (g - g0) % 2 == 1:
                        y_evac((g - 3) // 2)
                    if between and g == g0 + 11:
                        between()
                y_evac((g0 + 14) // 2)
                k["heads"] += 16

            def ffn(index, c0):
                T0 = k["ffn"] * FT
                pb = PA["ffn_dw"] + index * FT * 8

                def centre(t, a):
                    act.wait_ge(up_ready, t + (T0 + 1))
                    if not isinstance(t, int) or t >= 2:
                        act.wait_ge(prod_done, t + (T0 - 1))
                    for w in range(2):
                        def tap(n):
                            return par[:, bass.ds(t * 8 + (pb + 4 * w + n), 1)]
                        nc.scalar.activation(lin[:, a, w * S:(w + 1) * S], up_n[:, a, w * S:(w + 1) * S],
                                             ACT.Identity, bias=tap(3), scale=tap(1)).then_inc(lin_done, 1)

                def gelu(t, a):
                    act.wait_ge(taps_done, t * 4 + (4 * T0 + 3))
                    nc.scalar.activation(lin[:, a, 0:S], lin[:, a, 0:S], ACT.Gelu_apprx_tanh).then_inc(gelu_done, 1)

                def loop_split(i, a):
                    c = c0 + 1 + a
                    act.wait_ge(raw_full[c % RING], i * 16 + 16 * (c // RING + 1))
                    act.wait_ge(chunk_used, i * 3 + (c - RING + 1))
                    nc.scalar.activation(w_hi[:, c % RING, :], raw[:, c % RING, :], ACT.Copy).then_inc(hi_done, 1)

                if c0 == 0:
                    act.wait_ge(consts_loaded, 32)
                    split_hi(0)
                split_hi(c0 + 1, second=True)
                for t in range(0, 4, 2):
                    split_h((t, t + 1))
                    squares(x_pairs(t // 2, t // 2 + 1))
                split_h(range(4, DT))
                squares(x_pairs(2, 3))
                split_hi(c0 + 2)
                squares(x_pairs(3, 4))
                inv_sqrt()
                centre(0, 0)
                centre(1, 1)
                split_hi(c0 + 3)
                gelu(0, 0)
                gelu(1, 1)
                with act.Fori(1, FT // 2) as i:
                    loop_split(i, 0)
                    for a in range(2):
                        centre(i * 2 + a, a)
                        loop_split(i, 1 + a)
                        gelu(i * 2 + a, a)
                split_hi(c0 + 34)
                k["ffn"] += 1

            for name in stages:
                c0 = first_chunk[name]
                if name == "nat":
                    def table_part(n):
                        act.wait_ge(flipped, n + 1)
                        nc.scalar.activation(t_n[:, n * 512:(n + 1) * 512], bank[DOWN0 + n % 4][:, :], ACT.Copy)\
                                 .then_inc(table_step, 1)
                if not name.startswith("ffn"):
                    prenorm(c0)
                if name == "mix":
                    for c in range(9):
                        split_hi(c0 + c + 2)
                        src = bank[(c0 + c) % 3][:, :]
                        if c < 3:
                            evac(c0 + c, pair(lat, c), src)
                        elif c < 7:
                            evac(c0 + c, pair(qk_a, c - 3), src)
                        else:
                            evac(c0 + c, v_a[:, :, (c - 7) * S:(c - 6) * S], halves(src))
                        if c == 1:
                            squares([(lat[:, 0:2, :].rearrange("p a b -> p (a b)"), 512, evac_done, k["evac"]),
                                     (lat[:, 2, :], S, evac_done, k["evac"])])
                        elif c == 2:
                            squares([(lat[:, 3:5, :].rearrange("p a b -> p (a b)"), 512, evac_done, k["evac"])],
                                    k["sum"] - 1)
                            inv_sqrt()
                            split_h(range(8, 11))
                        elif c == 3:
                            inv_sqrt()
                            split_h(range(11, 13))
                    for c in range(9, 19):
                        if c < 17:
                            split_hi(c0 + c + 2)
                        src = bank[(c0 + c) % 3]
                        if c < 17:
                            dst = q_b if c < 13 else k_b
                            j = (c - 9) % 4
                            evac(c0 + c, dst[0:64, 2 * j:2 * j + 2, :], halves(src[0:64, :]))
                        else:
                            evac(c0 + c, v_b[:, :, (c - 17) * S:(c - 16) * S], halves(src[:, :]))
                    def y_squares(half):
                        y0 = 4 * half
                        squares([(y_att[:, t:t + 2, :].rearrange("p a b -> p (a b)"), 512, yev_done, t + 2)
                                 for t in (y0, y0 + 2)])

                    attention(between=lambda: y_squares(0))
                    y_squares(1)
                    inv_sqrt()
                    split_hi(c0 + 19)
                    split_h(range(4))
                    inv_sqrt()
                    split_h(range(4, 8))
                    split_hi(c0 + 20)
                    for c in range(19, 23):
                        split_hi(c0 + c + 2)
                        evac(c0 + c, pair(qk_a, c - 19), bank[(c0 + c) % 3][:, :])
                        squares([(pair(qk_a, c - 19), 512, evac_done, k["evac"])])
                    inv_sqrt()
                elif name.startswith("ffn"):
                    ffn(int(name[3:]), c0)
                    if name == "ffn0":
                        for t in range(4):
                            if t < 3:
                                act.wait_ge(sum_ready, t + 1)
                            else:
                                act.wait_ge(chunk_used, c0 + 33)
                            nc.scalar.activation(pair(y_post, t), bank[DOWN0 + t][:, :], ACT.Copy).then_inc(evac_done, 1)
                            k["evac"] += 1
                            if t < 2:
                                squares([(pair(y_post, t), 512, evac_done, k["evac"])])
                        squares([(pair(y_post, t), 512, evac_done, k["evac"] - 3 + t) for t in (2, 3)])
                        inv_sqrt()
                elif name.startswith("conv"):
                    j = int(name[4:])
                    for c in range(8):
                        split_hi(c0 + c + 2)
                        act.wait_ge(chunk_used, c0 + c + 1)
                        if k["gate"] >= 2:
                            act.wait_ge(glu_done, k["gate"] - 1)
                        nc.scalar.activation(c_sg[:, c % 2, :], bank[(c0 + c) % 3][:, S:2 * S], ACT.Sigmoid,
                                             bias=pcol("conv_b_in_2", 16 * j + 8 + c)).then_inc(gate_done, 1)
                        k["gate"] += 1
                    k["sum"] += 8
                    k["stat"] += 1
                    k["centred"] += 8
                    squares([(pair(c_acc, t), 512, centred, k["centred"] - 8 + 2 * t + 2) for t in range(4)])
                    inv_sqrt()
                    split_h(range(DT), silu=lambda t: pcol("conv_ln_b_2", 8 * j + t))
                    for c in range(8, 12):
                        split_hi(c0 + c + 2)
                elif name == "nat":
                    for n in range(4):
                        table_part(n)
                    for c in range(12):
                        split_hi(c0 + c + 2)
                        src = bank[(c0 + c) % 3][:, :]
                        if c < 8:
                            evac(c0 + c, pair(qk_n, c), src)
                            squares([(pair(qk_n, c), 512, evac_done, k["evac"])])
                            inv_sqrt(512)
                            table_part(4 + c)
                        else:
                            evac(c0 + c, v_n[:, :, (c - 8) * S:(c - 7) * S], halves(src))
                    attention()
                    for t in range(8):
                        act.wait_ge(yev_done, k["heads"] // 2 - 8 + t + 1)
                        nc.scalar.activation(h_hi[:, t, :], y_att[:, t, :], ACT.Copy).then_inc(hhi_done, 1)
                    for c in range(12, 16):
                        split_hi(c0 + c + 2)
                elif name == "ret":
                    nc.scalar.activation(dec[:, 0, :], par[:, PA["ret_log2_inv_decay_2"]:PA["ret_log2_inv_decay_2"] + 8],
                                         ACT.Exp, scale=-math.log(2.0)).then_inc(dec_a, 1)
                    act.wait_ge(dec_v, 1)
                    nc.scalar.activation(dec[:, 2, :], dec[:, 1, :], ACT.Ln).then_inc(dec_a, 1)
                    for c in range(8):
                        split_hi(c0 + c + 2)
                    for c in range(8, 16):
                        split_hi(c0 + c + 2)
                        evac(c0 + c, v_r[:, :, (c - 8) * S:(c - 7) * S], halves(bank[(c0 + c) % 3][:, :]))
                    for c in range(16, 24):
                        split_hi(c0 + c + 2)
                        evac(c0 + c, pair(g_r, c - 16), bank[(c0 + c) % 3][:, :], ACT.Silu)
                    sum0, centred0 = k["sum"], k["centred"]

                    def decays(h):
                        act.wait_ge(mask_v, 2 * h + 2)
                        nc.scalar.activation(d_r[:, h % 2, :], d_r[:, h % 2, :], ACT.Exp).then_inc(mask_a, 1)

                    def head_out(h):
                        for e in range(2):
                            act.wait_ge(ret_out, 2 * h + e + 1)
                            nc.scalar.activation((q_r, k_r)[e][:, 2 * h:2 * h + 2, :],
                                                 halves(bank[3 + 2 * (h % 2) + e][:, :]), ACT.Copy).then_inc(evac_done, 1)
                            k["evac"] += 1

                    def head_squares(h):
                        squares([((q_r, k_r)[e][:, 2 * h:2 * h + 2, :].rearrange("p a b -> p (a b)"), 512, centred,
                                  centred0 + 2 * h + 1 + e) for e in range(2)],
                                sum0 + 2 * RET_SUMS.index(("var", h - 1)) + 1 if h else sum0)

                    def head_norm(h, between=None):
                        inv_sqrt()
                        split_h(range(4 * h, 4 * h + 3))
                        if between:
                            between()
                        split_h([4 * h + 3])

                    decays(0)
                    decays(1)
                    head_out(0)
                    decays(2)
                    decays(3)
                    head_out(1)
                    head_squares(0)
                    head_out(2)
                    head_squares(1)
                    head_norm(0, lambda: head_out(3))
                    head_squares(2)
                    head_norm(1)
                    split_hi(c0 + 26)
                    split_hi(c0 + 27)
                    head_squares(3)
                    head_norm(2)
                    split_hi(c0 + 28)
                    split_hi(c0 + 29)
                    head_norm(3)
                    for c in range(30, 34):
                        split_hi(c0 + c)
                    k["sum"] = sum0 + 2 * len(RET_SUMS)
                    k["centred"] += 8
                k["x"] += 4

        @block.vector
        def _(dve):
            k = Counter()
            slot_free = [0, 0]

            def split_lo(c, second=False):
                if c >= n_chunks or c in second_chunks and not second:
                    return
                w, s = widths[c], c % RING
                dve.wait_ge(hi_done, c + 1)
                nc.vector.tensor_tensor(w_lo[:, s, 0:w], raw[:, s, 0:w], w_hi[:, s, 0:w].bitcast(F32), ALU.subtract)\
                         .then_inc(lo_done, 1)

            def root(n_sums, scale, width=S):
                k["sum"] += n_sums
                k["stat"] += 1
                v, y, t = rs_v[:, 0:width], rs_y[:, 0:width], rs_t[:, 0:width]
                dve.wait_ge(sum_done, k["sum"])
                if k["newton"]:
                    dve.wait_ge(newton, k["newton"])
                nc.vector.tensor_scalar(v, stat[:, 0:width], scale, EPS, ALU.mult, ALU.add).then_inc(stat_read, 1)
                k["ars"] += 1
                dve.wait_ge(ars_done, k["ars"])
                nc.vector.tensor_tensor(t, y, y, ALU.mult).then_inc(newton, 1)
                dve.wait_ge(newton, k["newton"] + 1)
                nc.vector.scalar_tensor_tensor(t, t, -0.5, v, ALU.mult, ALU.mult).then_inc(newton, 1)
                dve.wait_ge(newton, k["newton"] + 2)
                nc.vector.scalar_tensor_tensor(y, t, 1.5, y, ALU.add, ALU.mult).then_inc(newton, 1)
                k["newton"] += 3
                dve.wait_ge(newton, k["newton"])

            def normalize(sources, times=None, by_root=True):
                def lo(i):
                    slot, n_hhi, n_lo, t = pending[i]
                    dve.wait_ge(hhi_done, n_hhi)
                    nc.vector.tensor_tensor(h_lo[:, t, :], hn[:, slot, :], h_hi[:, t, :].bitcast(F32), ALU.subtract)\
                             .then_inc(hlo_done, 1)

                pending = []
                for i, (view, gain, t) in enumerate(sources):
                    slot = k["slot"] % 2
                    if slot_free[slot]:
                        dve.wait_ge(hlo_done, slot_free[slot])
                    if by_root:
                        first = nc.vector.scalar_tensor_tensor(hn[:, slot, :], view, gain, rs_y[:, 0:S], ALU.mult, ALU.mult)
                    else:
                        first = nc.vector.tensor_scalar(hn[:, slot, :], view, gain, None, ALU.mult)
                    if times:
                        first.then_inc(gated, 1)
                        k["gated"] += 1
                        dve.wait_ge(gated, k["gated"])
                        nc.vector.tensor_tensor(hn[:, slot, :], hn[:, slot, :], times(i), ALU.mult).then_inc(hn_done, 1)
                    else:
                        first.then_inc(hn_done, 1)
                    k["hhi"] += 1
                    k["hlo"] += 1
                    k["slot"] += 1
                    slot_free[slot] = k["hlo"]
                    pending.append((slot, k["hhi"], k["hlo"], t))
                    if i >= 1:
                        lo(i - 1)
                lo(len(pending) - 1)

            def prenorm(gain, c0):
                root(4, 1.0 / D)
                if c0 == 0:
                    split_lo(0)
                normalize([(x[:, t, :], gain(t), t) for t in range(DT)])
                split_lo(c0 + 1, second=True)

            def residual(c, t, src):
                dve.wait_ge(chunk_used, c + 1)
                nc.vector.tensor_tensor(pair(x, t), pair(x, t), src, ALU.add).then_inc(x_ready, 1)

            def residual_sums(c):
                for t in range(4):
                    if t < 3:
                        dve.wait_ge(sum_ready, k["whole"] + t + 1)
                    else:
                        dve.wait_ge(chunk_used, c + 1)
                    nc.vector.tensor_tensor(pair(x, t), pair(x, t), bank[DOWN0 + t][:, :], ALU.add).then_inc(x_ready, 1)
                k["whole"] += 3

            def post(y, gain):
                root(4, 1.0 / D)
                for t in range(DT + 1):
                    if t < DT:
                        nc.vector.scalar_tensor_tensor(y[:, t, :], y[:, t, :], gain(t), rs_y[:, 0:S], ALU.mult, ALU.mult)\
                                 .then_inc(post_step, 1)
                        k["post"] += 1
                    if t >= 1:
                        dve.wait_ge(post_step, k["post"] - (1 if t < DT else 0))
                        ins = nc.vector.tensor_tensor(x[:, t - 1, :], x[:, t - 1, :], y[:, t - 1, :], ALU.add)
                        if t % 2 == 0:
                            ins.then_inc(x_ready, 1)

            def attention(scale_of, bias_of):
                g0 = k["heads"]
                for g in range(g0, g0 + 17):
                    if g < g0 + 16:
                        h = g - g0
                        dve.wait_ge(score_done, g + 1)
                        if g >= 3:
                            dve.wait_ge(pt_done, g - 2)
                        s = sc_buf[:, g % 3, :]
                        bias, wait = bias_of(h)
                        if wait:
                            dve.wait_ge(*wait)
                        if bias is None:
                            nc.vector.tensor_scalar(s, bank[g % 2][:, :], scale_of(h), None, ALU.mult).then_inc(biased, 1)
                        elif len(bias) == 1:
                            nc.vector.scalar_tensor_tensor(s, bank[g % 2][:, :], scale_of(h), bias[0], ALU.mult, ALU.add)\
                                     .then_inc(biased, 1)
                        else:
                            for j in range(2):
                                ins = nc.vector.scalar_tensor_tensor(s[:, j * S:(j + 1) * S], bank[g % 2][:, j * S:(j + 1) * S],
                                                                     scale_of(h), bias[j], ALU.mult, ALU.add)
                            ins.then_inc(biased, 1)
                        dve.wait_ge(biased, 2 * g + 1)
                        if g >= 2:
                            dve.wait_ge(exp_done, 2 * (g - 2) + 2)
                        nc.vector.tensor_reduce(neg_max[:, 2 * (g % 2):2 * (g % 2) + 2], halves(s), AX.X, ALU.max, negate=True)\
                                 .then_inc(biased, 1)
                    if g > g0:
                        q = g - 1
                        zi = z_inv[:, 2 * (q % 2):2 * (q % 2) + 2]
                        dve.wait_ge(exp_done, 2 * q + 2)
                        nc.vector.reciprocal(zi, z_sum[:, 2 * (q % 2):2 * (q % 2) + 2]).then_inc(scaled, 1)
                        dve.wait_ge(scaled, 3 * q + 1)
                        for j in range(2):
                            s = sc_buf[:, q % 3, j * S:(j + 1) * S]
                            nc.vector.tensor_scalar(s, s, zi[:, j:j + 1], None, ALU.mult).then_inc(scaled, 1)
                k["heads"] += 16

            def ffn(index, c0, gain):
                T0 = k["ffn"] * FT
                pb = PA["ffn_dw"] + index * FT * 8

                def up_norm(t, a, bank_, used):
                    dve.wait_ge(chunk_used, used)
                    if not isinstance(t, int) or t >= 2:
                        dve.wait_ge(taps_done, t * 4 + (4 * T0 - 4))
                    nc.vector.tensor_tensor(halves(up_n[:, a, :]), halves(bank[bank_][:, :]),
                                            rs_y[:, 0:S].unsqueeze(1).broadcast_to([P, 2, S]), ALU.mult).then_inc(up_ready, 1)

                def taps(t, a):
                    for n in range(4):
                        w = n % 2
                        src, dst = up_n[:, a, w * S:(w + 1) * S], lin[:, a, w * S:(w + 1) * S]
                        if n < 2:
                            dve.wait_ge(lin_done, t * 2 + (2 * T0 + 2))
                            o, i_, tap = dst[:, 1:S], src[:, 0:S - 1], 0
                        else:
                            dve.wait_ge(taps_done, t * 4 + (4 * T0 + n - 1))
                            o, i_, tap = dst[:, 0:S - 1], src[:, 1:S], 2
                        nc.vector.scalar_tensor_tensor(o, i_, par[:, bass.ds(t * 8 + (pb + 4 * w + tap), 1)], o,
                                                       ALU.mult, ALU.add).then_inc(taps_done, 1)

                def gated_value(t, a):
                    dve.wait_ge(gelu_done, t + (T0 + 1))
                    dve.wait_ge(taps_done, t * 4 + (4 * T0 + 4))
                    if not isinstance(t, int) or t >= 2:
                        dve.wait_ge(ulo_done, t + (T0 - 1))
                    nc.vector.tensor_tensor(u32[:, a, :], lin[:, a, 0:S], lin[:, a, S:2 * S], ALU.mult).then_inc(prod_done, 1)

                def parts(t, a, d_used):
                    dve.wait_ge(prod_done, t + (T0 + 1))
                    dve.wait_ge(chunk_used, d_used)
                    nc.vector.tensor_copy(h_hi[:, 8 + a, :], u32[:, a, :]).then_inc(uhi_done, 1)
                    dve.wait_ge(uhi_done, t + (T0 + 1))
                    nc.vector.tensor_tensor(h_lo[:, 8 + a, :], u32[:, a, :], h_hi[:, 8 + a, :].bitcast(F32), ALU.subtract)\
                             .then_inc(ulo_done, 1)

                def loop_split(i, a):
                    c = c0 + 1 + a
                    dve.wait_ge(hi_done, i * 3 + (c + 1))
                    nc.vector.tensor_tensor(w_lo[:, c % RING, :], raw[:, c % RING, :], w_hi[:, c % RING, :].bitcast(F32),
                                            ALU.subtract).then_inc(lo_done, 1)

                if k["x"]:
                    dve.wait_ge(x_ready, k["x"])
                else:
                    split_lo(0)
                normalize([(x[:, t, :], gain(t), t) for t in range(DT)], by_root=False)
                split_lo(c0 + 1, second=True)
                split_lo(c0 + 2)
                root(4, 1.0 / D)
                up_norm(0, 0, c0 % 3, c0 + 1)
                up_norm(1, 1, (c0 + 1) % 3, c0 + 2)
                taps(0, 0)
                taps(1, 1)
                split_lo(c0 + 3)
                gated_value(0, 0)
                def two_tiles(i):
                    used = i * 3 + (c0 - 1)
                    parts(i * 2 + (-2), 0, used)
                    if not isinstance(i, int):
                        loop_split(i, -1)
                    loop_split(i, 0)
                    up_norm(i * 2, 0, (c0 + 2) % 3, i * 3 + c0)
                    gated_value(i * 2 + (-1), 1)
                    parts(i * 2 + (-1), 1, used)
                    taps(i * 2, 0)
                    up_norm(i * 2 + 1, 1, (c0 + 3) % 3, i * 3 + (c0 + 1))
                    loop_split(i, 1)
                    gated_value(i * 2, 0)
                    taps(i * 2 + 1, 1)

                two_tiles(1)
                with dve.Fori(2, FT // 2) as i:
                    two_tiles(i)
                parts(FT - 2, 0, c0 + 3 * (FT // 2) - 1)
                gated_value(FT - 1, 1)
                parts(FT - 1, 1, c0 + 3 * (FT // 2) - 1)
                split_lo(c0 + 33)
                split_lo(c0 + 34)
                k["ffn"] += 1

            dve.wait_ge(consts_loaded, 32)
            dve.wait_ge(x_loaded, 16)
            for name in stages:
                c0 = first_chunk[name]
                if name == "mix":
                    cos, sin = cc("rope_cos", S, 64, 96), cc("rope_sin", S, 96, 128)
                    cos2 = cos.unsqueeze(1).broadcast_to([32, 2, S])
                    sin2 = sin.unsqueeze(1).broadcast_to([32, 2, S])
                    prenorm(lambda t: pcol("norm_mix_pre", t), c0)
                    for c in range(9):
                        split_lo(c0 + c + 2)
                        k["evac"] += 1
                        if c == 2:
                            root(2, 1.0 / QL)
                            normalize([(lat[:, t, :], pcol("q_lat_norm", t), 8 + t) for t in range(3)])
                        elif c == 3:
                            root(1, 1.0 / KL)
                            normalize([(lat[:, 3 + t, :], pcol("kv_lat_norm", t), 11 + t) for t in range(2)])
                        elif c == 4:
                            dve.wait_ge(tables_loaded, 16)
                            dve.wait_ge(evac_done, k["evac"])
                            nc.vector.tensor_tensor(rope_t[64:96, 0, 0:S], lat[64:96, 5, :], cos, ALU.mult).then_inc(rope_step, 1)
                            nc.vector.tensor_tensor(rope_t[64:96, 1, 0:S], lat[96:128, 5, :], sin, ALU.mult).then_inc(rope_step, 1)
                            dve.wait_ge(rope_step, k["rope"] + 2)
                            nc.vector.tensor_tensor(k_b[64:96, :, :], rope_t[64:96, 0, 0:S].unsqueeze(1).broadcast_to([32, HB, S]),
                                                    rope_t[64:96, 1, 0:S].unsqueeze(1).broadcast_to([32, HB, S]), ALU.add)\
                                     .then_inc(rope_step, 1)
                            k["rope"] += 3
                    for c in range(9, 19):
                        if c < 17:
                            split_lo(c0 + c + 2)
                        k["evac"] += 1
                        if c < 13:
                            src = bank[(c0 + c) % 3]
                            dve.wait_ge(chunk_used, c0 + c + 1)
                            dve.wait_ge(rope_step, k["rope"])
                            nc.vector.tensor_tensor(halves(rope_t[64:96, 0, :]), halves(src[64:96, :]), cos2, ALU.mult)\
                                     .then_inc(rope_step, 1)
                            nc.vector.tensor_tensor(halves(rope_t[64:96, 1, :]), halves(src[96:128, :]), sin2, ALU.mult)\
                                     .then_inc(rope_step, 1)
                            dve.wait_ge(rope_step, k["rope"] + 2)
                            j = c - 9
                            nc.vector.tensor_tensor(q_b[64:96, 2 * j:2 * j + 2, :], halves(rope_t[64:96, 0, :]),
                                                    halves(rope_t[64:96, 1, :]), ALU.add).then_inc(rope_step, 1)
                            k["rope"] += 3
                    attention(lambda h: HDA ** -0.5 if h < HA else (NOPE + ROPE) ** -0.5,
                              lambda h: ([bias_a[:, h % 2, :]], (bias_full[h % 2], 16 * (h // 2 + 1))) if h < HA else (None, None))
                    for half, gain in enumerate(("out_norm_a", "out_norm_b")):
                        root(2, 1.0 / 512)
                        normalize([(y_att[:, t, :], pcol(gain, t % 4), t) for t in range(4 * half, 4 * half + 4)])
                        split_lo(c0 + 19 + half)
                    for c in range(19, 23):
                        split_lo(c0 + c + 2)
                    post(qk_a, lambda t: pcol("norm_mix_post", t))
                elif name.startswith("ffn"):
                    n = int(name[3:])
                    ffn(n, c0, (lambda t: pcol("norm_ffn_pre", t)) if n == 0 else (lambda t: pcol("norm2_g_2", 8 * (n - 1) + t)))
                    if n == 0:
                        k["whole"] += 3
                        post(y_post, lambda t: pcol("norm_ffn_post", t))
                    else:
                        residual_sums(c0 + 32)
                elif name.startswith("conv"):
                    j = int(name[4:])
                    layer = 3 * j
                    prenorm(lambda t: pcol("norm1_g_2", 8 * layer + t), c0)
                    last_tap = {}
                    k["pad"] += 2
                    dve.wait_ge(pad_done, k["pad"])

                    def glu(c):
                        split_lo(c0 + c + 2)
                        k["gate"] += 1
                        dve.wait_ge(gate_done, k["gate"])
                        nc.vector.scalar_tensor_tensor(u_pad[:, c, PADC:PADC + S], bank[(c0 + c) % 3][:, 0:S],
                                                       pcol("conv_b_in_2", 16 * j + c), c_sg[:, c % 2, :], ALU.add, ALU.mult)\
                                 .then_inc(glu_done, 1)
                        k["glu"] += 1

                    glu(0)
                    glu(1)
                    for p_ in range(4):
                        dve.wait_ge(glu_done, k["glu"])
                        steps = [(tap, m) for tap in range(CW) for m in (2 * p_, 2 * p_ + 1) if tap < CW - PE_TAPS[m]]
                        for n, (tap, m) in enumerate(steps):
                            if p_ < 3 and n == len(steps) // 3:
                                glu(2 * p_ + 2)
                            elif p_ < 3 and n == 2 * len(steps) // 3:
                                glu(2 * p_ + 3)
                            wcol = pcol("conv_dw_w_2", (8 * j + m) * CW + tap)
                            src = u_pad[:, m, tap:tap + S]
                            if tap == 0:
                                nc.vector.tensor_scalar(c_acc[:, m, :], src, wcol, pcol("conv_dw_b_2", 8 * j + m),
                                                        ALU.mult, ALU.add).then_inc(conv_step, 1)
                            else:
                                dve.wait_ge(conv_step, last_tap[m])
                                nc.vector.scalar_tensor_tensor(c_acc[:, m, :], src, wcol, c_acc[:, m, :],
                                                               ALU.mult, ALU.add).then_inc(conv_step, 1)
                            k["conv"] += 1
                            last_tap[m] = k["conv"]
                        k["pairs"] += 1
                        dve.wait_ge(pe_taps_done, k["pairs"])
                        for m in (2 * p_, 2 * p_ + 1):
                            dve.wait_ge(conv_step, last_tap[m])
                            nc.vector.tensor_tensor(c_acc[:, m, :], c_acc[:, m, :], half_bank(m), ALU.add).then_inc(conv_step, 1)
                            k["conv"] += 1
                    k["sum"] += 8
                    k["stat"] += 1
                    dve.wait_ge(sum_done, k["sum"])
                    nc.vector.tensor_scalar(rs_t[:, 0:S], stat[:, 0:S], 1.0 / D, None, ALU.mult).then_inc(stat_read, 1)
                    dve.wait_ge(stat_read, k["stat"])
                    for m in range(8):
                        nc.vector.tensor_tensor(c_acc[:, m, :], c_acc[:, m, :], rs_t[:, 0:S], ALU.subtract).then_inc(centred, 1)
                    k["centred"] += 8
                    root(4, 1.0 / D)
                    normalize([(c_acc[:, t, :], pcol("conv_ln_g_2", 8 * j + t), t) for t in range(DT)])
                    for c in range(8, 12):
                        split_lo(c0 + c + 2)
                        residual(c0 + c, c - 8, bank[(c0 + c) % 3][:, :])
                elif name == "nat":
                    prenorm(lambda t: pcol("norm1_g_2", 8 + t), c0)
                    for c in range(12):
                        split_lo(c0 + c + 2)
                        k["evac"] += 1
                        if c < 8:
                            root(1, 1.0 / NHD, 512)
                            gain = pcol("nat_q_norm_g_2" if c < 4 else "nat_k_norm_g_2")
                            nc.vector.scalar_tensor_tensor(pair(qk_n, c), pair(qk_n, c), gain, rs_y[:, :], ALU.mult, ALU.mult)\
                                     .then_inc(nq_done, 1)
                    dve.wait_ge(table_step, 12)
                    attention(lambda h: NHD ** -0.5,
                              lambda h: ([t_n[:, (6 * h + 2 - 2 * j) * GW:(6 * h + 6 - 2 * j) * GW] for j in range(2)], None))
                    for t in range(8):
                        k["hhi"] += 1
                        k["hlo"] += 1
                        dve.wait_ge(hhi_done, k["hhi"])
                        nc.vector.tensor_tensor(h_lo[:, t, :], y_att[:, t, :], h_hi[:, t, :].bitcast(F32), ALU.subtract)\
                                 .then_inc(hlo_done, 1)
                    for c in range(12, 16):
                        split_lo(c0 + c + 2)
                        residual(c0 + c, c - 12, bank[(c0 + c) % 3][:, :])
                elif name == "ret":
                    prenorm(lambda t: pcol("norm1_g_2", 16 + t), c0)
                    P_, W_, L_, D_, R_, E_, M_, G_ = (dec[:, n, :] for n in range(8))
                    dve.wait_ge(dec_a, 1)
                    nc.vector.tensor_scalar(W_, P_, -1.0, 1.0, ALU.mult, ALU.add).then_inc(dec_v, 1)
                    dve.wait_ge(dec_v, 1)
                    nc.vector.tensor_scalar(D_, W_, -1.0, 1.0, ALU.mult, ALU.add).then_inc(dec_v, 1)
                    dve.wait_ge(dec_v, 2)
                    nc.vector.tensor_scalar(D_, D_, 1e-30, None, ALU.max).then_inc(dec_v, 1)
                    dve.wait_ge(dec_v, 3)
                    nc.vector.reciprocal(R_, D_).then_inc(dec_v, 1)
                    nc.vector.tensor_scalar(E_, W_, 1.0, None, ALU.is_equal).then_inc(dec_v, 1)
                    dve.wait_ge(dec_v, 5)
                    nc.vector.tensor_tensor(E_, E_, P_, ALU.mult).then_inc(dec_v, 1)
                    dve.wait_ge(dec_a, 2)
                    nc.vector.tensor_tensor(M_, L_, P_, ALU.mult).then_inc(dec_v, 1)
                    dve.wait_ge(dec_v, 7)
                    nc.vector.tensor_tensor(M_, M_, R_, ALU.mult).then_inc(dec_v, 1)
                    dve.wait_ge(dec_v, 8)
                    nc.vector.tensor_tensor(G_, M_, E_, ALU.subtract).then_inc(dec_v, 1)
                    cos2 = cc("rot_cos", S).unsqueeze(1).broadcast_to([P, 2, S])
                    sin2 = cc("rot_sin", S).unsqueeze(1).broadcast_to([P, 2, S])
                    for c in range(8):
                        split_lo(c0 + c + 2)
                        dve.wait_ge(chunk_used, c0 + c + 1)
                        if c >= 2:
                            dve.wait_ge(rot_p, 2 * (c - 2) + 2)
                        src = halves(bank[(c0 + c) % 3][:, :])
                        nc.vector.tensor_tensor(halves(rot[:, 2 * (c % 2), :]), src, cos2, ALU.mult).then_inc(rot_v, 1)
                        nc.vector.tensor_tensor(halves(rot[:, 2 * (c % 2) + 1, :]), src, sin2, ALU.mult).then_inc(rot_v, 1)
                    for c in range(8, 24):
                        split_lo(c0 + c + 2)
                        k["evac"] += 1
                    dve.wait_ge(dec_v, 9)

                    def probs(h):
                        d = d_r[:, h % 2, :]
                        if h >= 2:
                            dve.wait_ge(prob_done, h - 1)
                        nc.vector.tensor_scalar(d, cc("fwd", 512), G_[:, h:h + 1], None, ALU.mult).then_inc(mask_v, 1)
                        dve.wait_ge(mask_v, 2 * h + 1)
                        nc.vector.scalar_tensor_tensor(d, cc("bwd", 512), G_[:, 4 + h:5 + h], d, ALU.mult, ALU.add)\
                                 .then_inc(mask_v, 1)
                        dve.wait_ge(mask_a, h + 1)
                        dve.wait_ge(score_done, k["heads"] + h + 1)
                        if h >= 2:
                            dve.wait_ge(ret_out, 2 * (h - 2) + 2)
                        nc.vector.scalar_tensor_tensor(p_r[:, h % 2, :], bank[h % 2][:, :], RKD ** -0.5, d, ALU.mult, ALU.mult)\
                                 .then_inc(prob_done, 1)

                    def centre(h):
                        k["sum"] += 2
                        dve.wait_ge(sum_done, k["sum"])
                        dve.wait_ge(newton, k["newton"])
                        if h:
                            dve.wait_ge(centred, k["centred"] + 2 * h)
                        nc.vector.tensor_scalar(rs_t[:, 0:S], bank[2][:, 0:S], 1.0 / RVD, None, ALU.mult).then_inc(mean_read, 1)
                        dve.wait_ge(mean_read, h + 1)
                        for e in range(2):
                            o = (q_r, k_r)[e][:, 2 * h:2 * h + 2, :]
                            nc.vector.tensor_tensor(o, o, rs_t[:, 0:S].unsqueeze(1).broadcast_to([P, 2, S]), ALU.subtract)\
                                     .then_inc(centred, 1)

                    def head_norm(h):
                        root(2, 1.0 / RVD)
                        normalize([(o_ret(h, e), pcol("ret_gn_g_2", 4 * h + e), 4 * h + e) for e in range(4)],
                                  times=lambda i: g_r[:, 4 * h + i, :])

                    probs(0)
                    probs(1)
                    probs(2)
                    centre(0)
                    probs(3)
                    centre(1)
                    head_norm(0)
                    centre(2)
                    centre(3)
                    head_norm(1)
                    split_lo(c0 + 26)
                    split_lo(c0 + 27)
                    head_norm(2)
                    split_lo(c0 + 28)
                    split_lo(c0 + 29)
                    head_norm(3)
                    for c in range(30, 34):
                        split_lo(c0 + c)
                    k["heads"] += 4
                    residual_sums(c0 + 31)
                k["x"] += 4

        @block.tensor
        def _(pe):
            k = Counter()
            ones, half_ones, ident = cc("ones", P), cc("half_ones", P), cc("ident", P)

            def product(dst, w_parts, x_parts, start, stop, **kw):
                nc.tensor.matmul(dst, w_parts[0], x_parts[0], start=start, stop=False, **kw)
                nc.tensor.matmul(dst, w_parts[1], x_parts[0], start=False, stop=False, **kw)
                return nc.tensor.matmul(dst, w_parts[0], x_parts[1], start=False, stop=stop, **kw)

            def weights(c, at, n=P):
                s = c % RING
                return w_hi[:, s, at:at + n], w_lo[:, s, at:at + n]

            def h_parts(t, a=0, n=S):
                return h_hi[:, t, a:a + n], h_lo[:, t, a:a + n]

            def feature_chunk(c, h0=0, n_k=8, n_m=2, wait_h=None, free=None, between=None):
                if free:
                    pe.wait_ge(*free)
                pe.wait_ge(lo_done, c + 1)
                steps = [(m, t) for m in range(n_m) for t in range(n_k)]
                if wait_h is not None:
                    steps = [(m, t) for t in range(n_k) for m in range(n_m)]
                for m, t in steps:
                    if wait_h is not None and m == 0:
                        pe.wait_ge(hlo_done, wait_h + t + 1)
                    last = product(bank[c % 3][:, m * S:(m + 1) * S], weights(c, (m * n_k + t) * P), h_parts(h0 + t),
                                   (m, t) == (0, 0), t == n_k - 1, skip_group_check=True)
                    if between and (m, t) == (1, 5):
                        between()
                last.then_inc(chunk_used, 1)

            def token_chunk(c, h0=0, n_k=8, free=None):
                if free:
                    pe.wait_ge(*free)
                pe.wait_ge(lo_done, c + 1)
                for j in range(2):
                    for t in range(n_k):
                        dst = bank[c % 3][:, j * S:(j + 1) * S]
                        a, b = h_parts(h0 + t, j * P, P)
                        w = weights(c, t * S, S)
                        nc.tensor.matmul(dst, a, w[0], start=t == 0, stop=False)
                        nc.tensor.matmul(dst, a, w[1], start=False, stop=False)
                        last = nc.tensor.matmul(dst, b, w[0], start=False, stop=t == n_k - 1)
                last.then_inc(chunk_used, 1)

            def sums(sources, matrix=None, width=S, start=True, stop=True):
                if k["stat"] and start:
                    pe.wait_ge(stat_read, k["stat"])
                matrix = ones if matrix is None else matrix
                n = len(sources)
                for i, (views, ready, value) in enumerate(sources):
                    pe.wait_ge(ready, value)
                    for v, view in enumerate(views):
                        last = nc.tensor.matmul(stat[:, 0:width], matrix, view, start=start and i == 0 and v == 0,
                                                stop=stop and i == n - 1 and v == len(views) - 1)
                    last.then_inc(sum_done, 1)
                k["stat"] += stop

            def sum_squares(widths_, matrix=None, start=True, stop=True):
                for_sum = []
                for w in widths_:
                    g = k["sq"]
                    k["sq"] += 1
                    if matrix is None:
                        views = [sq[:, g % 2, a:a + S] for a in range(0, w, S)]
                    else:
                        views = [sq[:, g % 2, 0:w]]
                    for_sum.append((views, sq_done, g + 1))
                sums(for_sum, matrix, S if matrix is None else widths_[0], start, stop)

            def down_chunk(c, slot_c, h0, first=False, last_=False, wait_h=()):
                pe.wait_ge(lo_done, c + 1)
                for m in range(8):
                    for a in range(2):
                        if m == 0 and wait_h:
                            pe.wait_ge(hlo_done, wait_h[a])
                        last = product(bank[DOWN0 + m // 2][:, (m % 2) * S:(m % 2 + 1) * S],
                                       weights(slot_c, a * D + m * P), h_parts(h0 + a),
                                       first and a == 0 and m % 2 == 0, last_ and a == 1, skip_group_check=True)
                    if last_ and m in (1, 3, 5):
                        last.then_inc(sum_ready, 1)
                last.then_inc(chunk_used, 1)

            def attention(scores, values, between=None):
                g0 = k["heads"]
                def score(g):
                    if g >= 2:
                        pe.wait_ge(biased, 2 * (g - 2) + 1)
                    for j in range(2):
                        q, key = scores(g - g0, j)
                        last = nc.tensor.matmul(bank[g % 2][:, j * S:(j + 1) * S], q, key, start=True, stop=True)
                    last.then_inc(score_done, 1)

                def transpose(g):
                    pe.wait_ge(scaled, 3 * g + 3)
                    if g >= 2:
                        pe.wait_ge(ptc_done, g - 1)
                    for kt in range(2):
                        for j in range(2):
                            last = nc.tensor.transpose(bank[2 + g % 2][:, kt * S + j * P:kt * S + (j + 1) * P],
                                                       sc_buf[:, g % 3, j * S + kt * P:j * S + (kt + 1) * P], ident)
                    last.then_inc(pt_done, 1)

                def value(g):
                    p_, side = g // 2, g % 2
                    pe.wait_ge(ptc_done, g + 1)
                    if side == 0 and p_ >= 2:
                        pe.wait_ge(yev_done, p_ - 1)
                    for kt in range(2):
                        last = nc.tensor.matmul(bank[4 + p_ % 2][64 * side:64 * side + 64, 0:S], values(g - g0, kt),
                                                pt_buf[:, g % 2, kt * S:(kt + 1) * S], start=kt == 0, stop=kt == 1)
                    last.then_inc(pv_done, 1)

                score(g0)
                score(g0 + 1)
                for g in range(g0, g0 + 16):
                    if g + 2 < g0 + 16:
                        score(g + 2)
                    transpose(g)
                    if g > g0:
                        value(g - 1)
                    if between and g == g0 + 11:
                        between()
                value(g0 + 15)
                k["heads"] += 16

            def ffn(c0):
                T0 = k["ffn"] * FT

                def up(t, c, slot_c):
                    pe.wait_ge(lo_done, c + 1)
                    if not isinstance(t, int) or t >= 3:
                        pe.wait_ge(up_ready, t + (T0 - 1))
                    for m in range(2):
                        for kt in range(8):
                            last = product(bank[slot_c % 3][:, m * S:(m + 1) * S], weights(slot_c, (8 * m + kt) * P),
                                           h_parts(kt), kt == 0, kt == 7)
                    last.then_inc(chunk_used, 1)

                def down(i, c, slot_c, first=False, last_=False):
                    pe.wait_ge(ulo_done, i * 2 + (T0 + 2))
                    down_chunk(c, slot_c, 8, first, last_)

                feature_chunk(c0, wait_h=k["hlo"], between=lambda: sum_squares([512] * 2, stop=False))
                sum_squares([512] * 2, start=False)
                up(1, c0 + 1, c0 + 1)
                up(2, c0 + 2, c0 + 2)
                up(3, c0 + 3, c0 + 3)
                down(0, c0 + 4, c0 + 4, first=True)
                with pe.Fori(2, FT // 2) as i:
                    for a in range(2):
                        up(i * 2 + a, i * 3 + (c0 - 1 + a), c0 + 2 + a)
                    down(i - 1, i * 3 + (c0 + 1), c0 + 4)
                down(FT // 2 - 1, c0 + 32, c0 + 32, last_=True)
                k["hlo"] += 8
                k["ffn"] += 1

            pe.wait_ge(consts_loaded, 32)
            for name in stages:
                c0 = first_chunk[name]
                if not name.startswith("ffn"):
                    sum_squares([512] * 4)
                e0 = k["evac"]
                if name == "mix":
                    for c in range(9):
                        free = (evac_done, e0 + c - 2) if c >= 3 else None
                        if c >= 7:
                            token_chunk(c0 + c, free=free)
                        else:
                            feature_chunk(c0 + c, wait_h=k["hlo"] if c == 0 else None, free=free)
                        if c == 2:
                            sum_squares([512, S])
                        elif c == 3:
                            sum_squares([512])
                    k["hlo"] += 8
                    for c in range(9, 19):
                        free = (evac_done, e0 + c - 2)
                        if 12 <= c < 16:
                            pe.wait_ge(rope_step, 3 * (c - 12) + 5)
                        if c < 13:
                            feature_chunk(c0 + c, 8, 3, 2, k["hlo"] if c == 9 else None, free)
                        elif c < 17:
                            feature_chunk(c0 + c, 11, 2, 2, k["hlo"] + 3 if c == 13 else None, free)
                        else:
                            token_chunk(c0 + c, 11, 2, free)
                    k["hlo"] += 5
                    k["evac"] += 19
                    pe.wait_ge(evac_done, k["evac"])
                    def mix_scores(h, j):
                        if h < HA:
                            r = slice(64 * (h % 2), 64 * (h % 2) + 64)
                            return qk_a[r, h // 2, j * P:(j + 1) * P], qk_a[r, 4 + h // 2, :]
                        if (h, j) == (HA, 0):
                            pe.wait_ge(rope_step, 15)
                        h -= HA
                        return q_b[0:96, h, j * P:(j + 1) * P], k_b[0:96, h, :]

                    attention(mix_scores, lambda h, kt: (v_a if h < HA else v_b)[:, kt, 64 * (h % 8):64 * (h % 8) + 64],
                              between=lambda: sum_squares([512] * 2))
                    sum_squares([512] * 2)
                    for c in range(19, 23):
                        feature_chunk(c0 + c, wait_h=k["hlo"] if c == 19 else None,
                                      free=(evac_done, k["evac"] + 1) if c == 22 else None)
                    k["hlo"] += 8
                    k["evac"] += 4
                    sum_squares([512] * 4)
                elif name.startswith("ffn"):
                    ffn(c0)
                    if name == "ffn0":
                        sum_squares([512] * 4)
                        k["evac"] += 4
                elif name.startswith("conv"):
                    def tap_products(p_):
                        pe.wait_ge(glu_done, k["glu"] + 2 * p_ + 2)
                        for m in (2 * p_, 2 * p_ + 1):
                            pe.wait_ge(diag_done, k["diag"] + m + 1)
                            for tap in pe_taps(m):
                                last = nc.tensor.matmul(half_bank(m), diag[:, diag_slot(m, tap), :], u_pad[:, m, tap:tap + S],
                                                        start=tap == CW - PE_TAPS[m], stop=tap == CW - 1)
                        last.then_inc(pe_taps_done, 1)

                    if k["x"]:
                        pe.wait_ge(x_ready, k["x"])
                    for c in range(8):
                        feature_chunk(c0 + c, wait_h=k["hlo"] if c == 0 else None,
                                      free=(glu_done, k["glu"] + c - 2) if c >= 3 else None)
                        if c >= 3 and c % 2:
                            tap_products(c // 2 - 1)
                    tap_products(3)
                    k["glu"] += 8
                    k["hlo"] += 8
                    k["diag"] += 8
                    n_steps = [sum(CW - PE_TAPS[n] + 1 for n in range(m // 2 * 2 + 2)) for m in range(8)]
                    sums([([c_acc[:, m, :]], conv_step, k["conv"] + n_steps[m]) for m in range(8)])
                    k["conv"] += n_steps[7]
                    sum_squares([512] * 4)
                    for c in range(8, 12):
                        feature_chunk(c0 + c, wait_h=k["hlo"] if c == 8 else None,
                                      free=(x_ready, k["x"] + 1) if c == 11 else None)
                    k["hlo"] += 8
                elif name == "nat":
                    def flip(n):
                        pe.wait_ge(table_masked, n + 1)
                        if n >= 4:
                            pe.wait_ge(table_step, n - 3)
                        nc.tensor.matmul(bank[DOWN0 + n % 4][:, :], cc("flip", P), t_up[:, n * 512:(n + 1) * 512],
                                         start=True, stop=True).then_inc(flipped, 1)

                    for n in range(4):
                        flip(n)
                    for c in range(12):
                        free = (evac_done, e0 + c - 2) if c >= 3 else None
                        if c < 8:
                            feature_chunk(c0 + c, wait_h=k["hlo"] if c == 0 else None, free=free)
                        else:
                            token_chunk(c0 + c, free=free)
                        if 1 <= c <= 8:
                            sum_squares([512], half_ones)
                        if c < 8:
                            flip(4 + c)
                    k["hlo"] += 8
                    k["evac"] += 12
                    pe.wait_ge(evac_done, k["evac"])
                    pe.wait_ge(nq_done, 8)

                    def nat_scores(h, j):
                        r = slice(64 * (h % 2), 64 * (h % 2) + 64)
                        return qk_n[r, h // 2, j * P:(j + 1) * P], qk_n[r, 8 + h // 2, :]

                    attention(nat_scores, lambda h, kt: v_n[:, kt, 64 * h:64 * h + 64])
                    for c in range(12, 16):
                        feature_chunk(c0 + c, wait_h=k["hlo"] if c == 12 else None,
                                      free=(x_ready, k["x"] + 1) if c == 15 else None)
                    k["hlo"] += 8
                elif name == "ret":
                    for c in range(24):
                        if c < 3:
                            free = None
                        elif c < 11:
                            free = (rot_v, 2 * (c - 3) + 2)
                        else:
                            free = (evac_done, e0 + c - 10)
                        if 8 <= c < 16:
                            token_chunk(c0 + c, free=free)
                        else:
                            feature_chunk(c0 + c, wait_h=k["hlo"] if c == 0 else None, free=free)
                    k["hlo"] += 8
                    k["evac"] += 16
                    pe.wait_ge(evac_done, k["evac"])
                    pe.wait_ge(rot_p, 16)

                    def score(h):
                        if h >= 2:
                            pe.wait_ge(prob_done, h - 1)
                        for jt in range(2):
                            for d in range(2):
                                last = nc.tensor.matmul(bank[h % 2][:, jt * S:(jt + 1) * S],
                                                        k_r[:, 2 * h + d, jt * P:(jt + 1) * P], q_r[:, 2 * h + d, :],
                                                        start=d == 0, stop=d == 1)
                        last.then_inc(score_done, 1)

                    def output(h):
                        pe.wait_ge(prob_done, h + 1)
                        if h >= 2:
                            pe.wait_ge(evac_done, k["evac"] + 2 * (h - 2) + 2)
                        for e in range(4):
                            for jt in range(2):
                                last = nc.tensor.matmul(bank[3 + 2 * (h % 2) + e // 2][:, (e % 2) * S:(e % 2 + 1) * S],
                                                        v_r[:, jt, h * RVD + e * P:h * RVD + (e + 1) * P],
                                                        p_r[:, h % 2, jt * S:(jt + 1) * S], start=jt == 0, stop=jt == 1)
                            if e % 2:
                                last.then_inc(ret_out, 1)

                    def mean(h):
                        if h:
                            pe.wait_ge(mean_read, h)
                        for e in range(2):
                            pe.wait_ge(evac_done, k["evac"] + 2 * h + e + 1)
                            for n in range(2):
                                last = nc.tensor.matmul(bank[2][:, 0:S], ones, o_ret(h, 2 * e + n), start=e + n == 0, stop=e + n == 2)
                            last.then_inc(sum_done, 1)

                    def var(h):
                        sum_squares([512] * 2)

                    def project(n):
                        down_chunk(c0 + 24 + n, c0 + 24 + n, 2 * n, n == 0, n == 7, [k["hlo"] + 2 * n + 1, k["hlo"] + 2 * n + 2])

                    score(0)
                    score(1)
                    output(0)
                    score(2)
                    mean(0)
                    output(1)
                    score(3)
                    mean(1)
                    output(2)
                    var(0)
                    output(3)
                    mean(2)
                    mean(3)
                    var(1)
                    project(0)
                    project(1)
                    var(2)
                    project(2)
                    project(3)
                    var(3)
                    for n in range(4, 8):
                        project(n)
                    k["heads"] += 4
                    k["evac"] += 8
                    k["hlo"] += 16
                k["x"] += 4


def split_columns(w, cols):
    return w[:, cols].reshape(w.shape[0] // P, P, len(cols)).transpose(1, 0, 2)


def pack_weights(a, stages=ALL_STAGES):
    n = sum(len(chunk_widths(s)) for s in stages) + 1
    out = np.zeros((n, P, CH), np.float32)
    at = 0

    def put(*blocks):
        nonlocal at
        flat = np.concatenate([b.reshape(P, -1) for b in blocks], 1)
        out[at, :, :flat.shape[1]] = flat
        at += 1

    def tiles(w, *cols):
        put(*[split_columns(w, c) for c in cols])

    def span(a0, n=P):
        return np.arange(a0, a0 + n)

    def columns(w, n_chunks):
        for c in range(n_chunks):
            tiles(w, span(2 * c * P), span((2 * c + 1) * P))

    for s in stages:
        if s == "mix":
            w = a["w_in"][0]
            q0, kv0, r0 = 3 * 512, 3 * 512 + QL, 3 * 512 + QL + KL
            swap = np.concatenate([np.arange(16, 32), np.arange(16)])
            key = np.concatenate([np.arange(32), np.arange(32), np.arange(32), swap]) + r0
            tiles(w, span(q0), span(q0 + P))
            tiles(w, span(q0 + 2 * P), span(kv0))
            tiles(w, span(kv0 + P), key)
            columns(w, 4)
            for c in range(2):
                tiles(w, span(2 * 512 + c * 256, 256))
            head = np.concatenate([np.arange(NOPE + ROPE), NOPE + swap])
            for c in range(4):
                tiles(a["w_uq"][0], *[(NOPE + ROPE) * h + head for h in (2 * c, 2 * c + 1)])
            for c in range(4):
                tiles(a["w_ukv"][0], *[span(P * h) for h in (2 * c, 2 * c + 1)])
            values = np.concatenate([span(P * h + 64, 64) for h in range(HB)])
            for c in range(2):
                tiles(a["w_ukv"][0], values[256 * c:256 * c + 256])
            columns(a["w_o"][0], 4)
        elif s.startswith("ffn"):
            i = int(s[3:])
            up = a["w_up"][0] if i == 0 else a["ffn_w_up_2"][i - 1]
            down = a["w_down"][0] if i == 0 else a["ffn_w_down_2"][i - 1]
            ups = up.reshape(8, P, 2, FT, P)[:, :, ::-1 if i else 1]
            ups = ups.transpose(3, 1, 2, 0, 4).reshape(FT, P, CH)
            downs = down.reshape(FT // 2, 2, P, D).transpose(0, 2, 1, 3).reshape(FT // 2, P, CH)
            order = [ups[0], ups[1]]
            for b in range(1, FT // 2):
                order += [ups[2 * b], ups[2 * b + 1], downs[b - 1]]
            order.append(downs[FT // 2 - 1])
            for block_ in order:
                out[at] = block_
                at += 1
        elif s.startswith("conv"):
            j = int(s[4:])
            w = a["conv_w_in_2"][j]
            for m in range(8):
                tiles(w, span(m * P), span(D + m * P))
            columns(a["conv_w_out_2"][j], 4)
        elif s == "nat":
            w = a["nat_w_qkv_2"][0]
            columns(w, 8)
            for c in range(4):
                tiles(w, span(2 * D + 256 * c, 256))
            columns(a["nat_w_out_2"][0], 4)
        else:
            w = a["ret_w_in_2"][0]
            for h in range(RH):
                for part in range(2):
                    tiles(w, span(part * D + 2 * h * P), span(part * D + (2 * h + 1) * P))
            for c in range(8):
                tiles(w, span(2 * D + 256 * c, 256))
            for c in range(8):
                tiles(w, span(2 * D + 2048 + 2 * c * P), span(2 * D + 2048 + (2 * c + 1) * P))
            for block_ in a["ret_w_out_2"][0].reshape(8, 2, P, D).transpose(0, 2, 1, 3).reshape(8, P, CH):
                out[at] = block_
                at += 1
    assert at == n - 1
    return out


def pack_params(a):
    at, n = param_layout()
    out = np.zeros((P, n), np.float32)

    def put(name, v):
        v = v.reshape(-1, P).T
        out[:, at[name]:at[name] + v.shape[1]] = v

    for name in ("norm_mix_pre", "q_lat_norm", "kv_lat_norm", "out_norm_a", "out_norm_b", "norm_mix_post", "norm_ffn_pre",
                 "norm_ffn_post", "norm1_g_2", "norm2_g_2", "conv_b_in_2", "conv_dw_b_2", "conv_ln_g_2", "conv_ln_b_2",
                 "ret_gn_g_2"):
        put(name, a[name])
    put("conv_dw_w_2", a["conv_dw_w_2"].reshape(2, CW, 8, P).transpose(0, 2, 1, 3))
    for name in ("nat_q_norm_g_2", "nat_k_norm_g_2"):
        put(name, np.tile(a[name], (1, 2)))
    o = at["ret_log2_inv_decay_2"]
    out[:, o:o + 8] = a["ret_log2_inv_decay_2"].reshape(1, 8)
    taps = np.concatenate([a["conv_w"], a["ffn_dw_w_2"]]).reshape(5, 3, 2, FT, P)
    bias = np.concatenate([a["conv_b"], a["ffn_dw_b_2"]]).reshape(5, 1, 2, FT, P)
    both = np.concatenate([taps, bias], 1).transpose(0, 3, 2, 1, 4)
    put("ffn_dw", np.concatenate([both[:1], both[1:, :, ::-1]]))
    return out


def lay_out(inputs, stages=ALL_STAGES):
    a = {name: np.asarray(v) for name, v in inputs.items()}
    rpb = np.zeros((NH, 15, P), np.float32)
    rpb[:, :, GW - KW:GW + KW - 1] = a["nat_rpb_2"][0]
    return {
        "wstream": pack_weights(a, stages),
        "x_in": np.ascontiguousarray(a["x"][0].T.reshape(DT, P, S)),
        "params": pack_params(a),
        "consts": build_constants(),
        "dilated_bias": dilated_bias(),
        "rpb": rpb,
    }


def declare(nc, arrays, stages=ALL_STAGES):
    args = [nc.dram_tensor(name, v.shape, F32, kind="ExternalInput").ap() for name, v in arrays.items()]
    args.append(nc.dram_tensor("x_out", (DT, P, S), F32, kind="ExternalOutput").ap())
    build_program(nc, *args, stages=stages)


def kernel(**inputs):
    import concourse.bacc as bacc
    from concourse.bass_utils import run_bass_kernel_spmd

    arrays = lay_out(inputs)
    nc = bacc.Bacc("TRN2", target_bir_lowering=False, num_devices=1)
    declare(nc, arrays)
    r = run_bass_kernel_spmd(nc, [arrays], core_ids=[0])
    return np.ascontiguousarray(r.results[0]["x_out"].reshape(1, D, S).transpose(0, 2, 1))
```
